# Optimizing a Trainium2 kernel written in Bass

```python
import jax, jax.numpy as jnp
from jax import lax
import numpy as np

D_MODEL = 1024
BATCH = 1
SEQ = 256
DEPTH = 2

CHUNK = 64
N_A_LAYERS = DEPTH // 2
N_B_LAYERS = DEPTH - N_A_LAYERS
HEAD_DIM = 64
MIX_WIDTH = D_MODEL
MEM_HEADS = 4
MEM_WIDTH = MEM_HEADS * HEAD_DIM
MIXER_WIDTH = MIX_WIDTH - MEM_WIDTH
POOL_WINDOWS = (2, 4, 8, 16)
POOL_GROUPS = len(POOL_WINDOWS)
POOL_GROUP_WIDTH = MIXER_WIDTH // POOL_GROUPS
ATTN_HEADS = MIXER_WIDTH // HEAD_DIM
KV_HEADS = 4
GQA_GROUP = ATTN_HEADS // KV_HEADS
WINDOW = 128
WINDOW_CHUNKS = WINDOW // CHUNK
ROT_DIM = HEAD_DIM // 4
ROPE_THETA = 500000.0
D_FF = ((8 * D_MODEL // 3 + 127) // 128) * 128
N_MEM = 256
EPS = 1e-6
NEG_INF = -1e30

kernel_name = 'hybrid_pool_swa_sink_yoco_encoder'

def rms_norm(x, g):
    xf = x.astype(jnp.float32)
    y = xf * lax.rsqrt(jnp.mean(xf * xf, axis=-1, keepdims=True) + EPS)
    return (y * g.astype(jnp.float32)).astype(x.dtype)

def swiglu_half_step(h, norm_g, w_gate_up, w_down):
    hn = rms_norm(h, norm_g)
    gate, up = jnp.split(hn @ w_gate_up, 2, axis=-1)
    return h + 0.5 * ((jax.nn.silu(gate) * up) @ w_down)

def rope_tables(positions):
    inv_freq = ROPE_THETA ** (-jnp.arange(0, ROT_DIM, 2, dtype=jnp.float32) / ROT_DIM)
    ang = positions.astype(jnp.float32)[..., None] * inv_freq
    return jnp.cos(ang)[:, :, None, :], jnp.sin(ang)[:, :, None, :]

def partial_rope(x, cos, sin):
    xr = x[..., :ROT_DIM].astype(jnp.float32)
    x1, x2 = xr[..., :ROT_DIM // 2], xr[..., ROT_DIM // 2:]
    rot = jnp.concatenate([x1 * cos - x2 * sin, x2 * cos + x1 * sin], axis=-1).astype(x.dtype)
    return jnp.concatenate([rot, x[..., ROT_DIM:]], axis=-1)

def multiscale_pool_mixer(u, w_groups, scale):
    B, S, _ = u.shape
    g = u.reshape(B, S, POOL_GROUPS, POOL_GROUP_WIDTH).astype(jnp.float32)
    cs = jnp.concatenate([jnp.zeros((B, 1, POOL_GROUPS, POOL_GROUP_WIDTH), jnp.float32),
                          jnp.cumsum(g, axis=1)], axis=1)
    t = jnp.arange(S, dtype=jnp.int32)
    windows = jnp.array(POOL_WINDOWS, dtype=jnp.int32)
    lo_idx = jnp.maximum(t[:, None] + 1 - windows[None, :], 0)
    lo = cs[:, lo_idx, jnp.arange(POOL_GROUPS)[None, :], :]
    cnt = (t[:, None] + 1 - lo_idx).astype(jnp.float32)
    pooled = (cs[:, 1:] - lo) / cnt[None, :, :, None] - g
    y = jnp.einsum('bsgc,gcd->bsgd', pooled.astype(u.dtype), w_groups)
    return y.reshape(B, S, MIXER_WIDTH) * scale

def banded_sink_attention(q, k, v, sinks):
    B, S, _, d = q.shape
    n_c = S // CHUNK
    qc = q.reshape(B, n_c, CHUNK, KV_HEADS, GQA_GROUP, d)

    def band(t):
        tc = t.reshape(B, n_c, CHUNK, KV_HEADS, d)
        padded = jnp.pad(tc, ((0, 0), (WINDOW_CHUNKS - 1, 0), (0, 0), (0, 0), (0, 0)))
        return jnp.concatenate([padded[:, j:j + n_c] for j in range(WINDOW_CHUNKS)], axis=2)

    kb, vb = band(k), band(v)
    logits = jnp.einsum('bcqkgd,bcskd->bckgqs', qc, kb).astype(jnp.float32) * (d ** -0.5)
    c_idx = jnp.arange(n_c)[:, None]
    s_idx = jnp.arange(WINDOW_CHUNKS * CHUNK)[None, :]
    valid = (c_idx - (WINDOW_CHUNKS - 1) + s_idx // CHUNK) >= 0
    logits = jnp.where(valid[None, :, None, None, None, :], logits, NEG_INF)
    sink = jnp.broadcast_to(sinks.astype(jnp.float32).reshape(1, 1, KV_HEADS, GQA_GROUP, 1, 1),
                            logits.shape[:-1] + (1,))
    p = jax.nn.softmax(jnp.concatenate([logits, sink], axis=-1), axis=-1)[..., :-1]
    out = jnp.einsum('bckgqs,bcskd->bcqkgd', p.astype(v.dtype), vb)
    return out.reshape(B, S, ATTN_HEADS * d)

def memory_attention(q, mem, mem_norm_g, w_mem_kv, q_norm_g, k_norm_g):
    B, M, _ = mem.shape
    kv = rms_norm(mem, mem_norm_g) @ w_mem_kv
    k, v = jnp.split(kv.reshape(B, M, 2 * MEM_HEADS, HEAD_DIM), 2, axis=2)
    q = rms_norm(q, q_norm_g)
    k = rms_norm(k, k_norm_g)
    logits = jnp.einsum('bshd,bmhd->bhsm', q, k).astype(jnp.float32) * (HEAD_DIM ** -0.5)
    p = jax.nn.softmax(logits, axis=-1)
    out = jnp.einsum('bhsm,bmhd->bshd', p.astype(v.dtype), v)
    return out.reshape(B, q.shape[1], MEM_WIDTH)

def setup_inputs(seed: int = 0) -> dict:
    key = jax.random.key(seed)
    ks = jax.random.split(key, 26)

    def nrm(k, shape, fan_in):
        return jax.random.normal(k, shape, jnp.float32) * (fan_in ** -0.5)

    def gain(k, shape):
        return 1.0 + 0.05 * jax.random.normal(k, shape, jnp.float32)

    start = jax.random.randint(ks[2], (BATCH, 1), 0, 4096, dtype=jnp.int32) * CHUNK
    positions = (start + jnp.arange(SEQ, dtype=jnp.int32)[None, :]).astype(jnp.int32)
    return {
        'x': jax.random.normal(ks[0], (BATCH, SEQ, D_MODEL), jnp.float32),
        'mem': jax.random.normal(ks[1], (BATCH, N_MEM, D_MODEL), jnp.float32),
        'positions': positions,
        'ffn1_norm': gain(ks[3], (DEPTH, D_MODEL)),
        'ffn1_w_gate_up': nrm(ks[4], (DEPTH, D_MODEL, 2 * D_FF), D_MODEL),
        'ffn1_w_down': nrm(ks[5], (DEPTH, D_FF, D_MODEL), D_FF),
        'mix_norm': gain(ks[6], (DEPTH, D_MODEL)),
        'w_in': nrm(ks[7], (DEPTH, D_MODEL, MIX_WIDTH), D_MODEL),
        'w_out': nrm(ks[8], (DEPTH, MIX_WIDTH, D_MODEL), MIX_WIDTH),
        'pool_w': nrm(ks[9], (N_A_LAYERS, POOL_GROUPS, POOL_GROUP_WIDTH, POOL_GROUP_WIDTH), POOL_GROUP_WIDTH),
        'pool_scale': gain(ks[10], (N_A_LAYERS, MIXER_WIDTH)),
        'attn_q_norm': gain(ks[11], (N_B_LAYERS, HEAD_DIM)),
        'attn_sinks': 0.5 * jax.random.normal(ks[12], (N_B_LAYERS, ATTN_HEADS), jnp.float32),
        'kv_norm': gain(ks[13], (D_MODEL,)),
        'w_kv': nrm(ks[14], (D_MODEL, 2 * KV_HEADS * HEAD_DIM), D_MODEL),
        'k_norm': gain(ks[15], (HEAD_DIM,)),
        'mem_norm': gain(ks[16], (DEPTH, D_MODEL)),
        'w_mem_kv': nrm(ks[17], (DEPTH, D_MODEL, 2 * MEM_WIDTH), D_MODEL),
        'mem_q_norm': gain(ks[18], (DEPTH, HEAD_DIM)),
        'mem_k_norm': gain(ks[19], (DEPTH, HEAD_DIM)),
        'ffn2_norm': gain(ks[20], (DEPTH, D_MODEL)),
        'ffn2_w_gate_up': nrm(ks[21], (DEPTH, D_MODEL, 2 * D_FF), D_MODEL),
        'ffn2_w_down': nrm(ks[22], (DEPTH, D_FF, D_MODEL), D_FF),
    }

def reference(x, mem, positions, ffn1_norm, ffn1_w_gate_up, ffn1_w_down, mix_norm, w_in, w_out,
              pool_w, pool_scale, attn_q_norm, attn_sinks, kv_norm, w_kv, k_norm,
              mem_norm, w_mem_kv, mem_q_norm, mem_k_norm, ffn2_norm, ffn2_w_gate_up, ffn2_w_down):
    B, S, _ = x.shape
    cos, sin = rope_tables(positions)
    h = x
    k_shared = v_shared = None
    for i in range(DEPTH):
        if i == N_A_LAYERS:
            kv = (rms_norm(h, kv_norm) @ w_kv).reshape(B, S, 2 * KV_HEADS, HEAD_DIM)
            k_shared, v_shared = jnp.split(kv, 2, axis=2)
            k_shared = partial_rope(rms_norm(k_shared, k_norm), cos, sin)
        h = swiglu_half_step(h, ffn1_norm[i], ffn1_w_gate_up[i], ffn1_w_down[i])
        z = rms_norm(h, mix_norm[i]) @ w_in[i]
        z_mix, z_mem = z[..., :MIXER_WIDTH], z[..., MIXER_WIDTH:]
        if i < N_A_LAYERS:
            y_mix = multiscale_pool_mixer(z_mix, pool_w[i], pool_scale[i])
        else:
            j = i - N_A_LAYERS
            q = rms_norm(z_mix.reshape(B, S, ATTN_HEADS, HEAD_DIM), attn_q_norm[j])
            q = partial_rope(q, cos, sin)
            y_mix = banded_sink_attention(q, k_shared, v_shared, attn_sinks[j])
        y_mem = memory_attention(z_mem.reshape(B, S, MEM_HEADS, HEAD_DIM), mem, mem_norm[i],
                                 w_mem_kv[i], mem_q_norm[i], mem_k_norm[i])
        h = h + jnp.concatenate([y_mix, y_mem], axis=-1) @ w_out[i]
        h = swiglu_half_step(h, ffn2_norm[i], ffn2_w_gate_up[i], ffn2_w_down[i])
    return h


_drawn_inputs = setup_inputs


def setup_inputs(seed=0):
    import zlib

    import numpy as np

    out = dict(_drawn_inputs(seed))
    spreads = {}
    factors = {'attn_q_norm': 8.0,
     'attn_sinks': 8.0,
     'kv_norm': 7.912,
     'k_norm': 8.0,
     'mem_norm': 8.0,
     'mem_q_norm': 8.0,
     'mem_k_norm': 8.0}
    for name, (base, spread) in spreads.items():
        noise = np.random.default_rng([zlib.crc32(name.encode()), seed]).standard_normal(out[name].shape)
        drawn = base * np.exp(spread * noise) if base else spread * noise
        out[name] = __import__('jax').numpy.asarray(drawn.astype(out[name].dtype))
    for name, factor in factors.items():
        out[name] = (out[name] * factor).astype(out[name].dtype)
    return out
```

```python
from contextlib import ExitStack

import numpy as np

import concourse.bass as bass
from concourse import mybir

F32 = mybir.dt.float32
F32R = mybir.dt.float32r
I32 = mybir.dt.int32
ALU = mybir.AluOpType
ACT = mybir.ActivationFunctionType
AX = mybir.AxisListType

P = 128
D = 1024
S = 256
NT = S // P
KC = D // P
FF = ((8 * D // 3 + 127) // 128) * 128
FB = 256
STEPS = FF // FB
HD = 64
MIXER = 768
NHA = MIXER // HD
KVH = 4
GQA = NHA // KVH
MEMH = 4
GROUPS = 4
GW = MIXER // GROUPS
GC = GW // 2
WINDOWS = (2, 4, 8, 16)
CHUNK = 64
ROT = HD // 4
RH = ROT // 2
EPS = 1e-6
NEG_INF = -1e30
SM_SCALE = HD ** -0.5
SLOTS = 3
MAGIC = 1.5 * 2.0 ** 23

SUM_BANK = 0
GU_BANK = 4
TR_BANK = 6
PT_BANK = 3
O_BANK = 6


def two_pi_parts():
    a = np.floor(2 * np.pi * 2 ** 9) / 2 ** 9
    b = np.floor((2 * np.pi - a) * 2 ** 22) / 2 ** 22
    return float(a), float(b), float(2 * np.pi - a - b)


FFN_UNITS = 3 * STEPS
UNIT = {}
_u = 0
for _name, _n in (("ffn0", FFN_UNITS), ("mkv0", 2), ("z0", 4), ("out0", 4), ("ffn1", FFN_UNITS), ("kv", 2),
                  ("ffn2", FFN_UNITS), ("mkv1", 2), ("z1", 4), ("out1", 4), ("ffn3", FFN_UNITS)):
    UNIT[_name] = _u
    _u += _n
UNITS = _u

NORMS = [("h", "main"), ("mem", "side"), ("h", "main"), ("h", "main"), ("h", "side"), ("h", "main"),
         ("mem", "side"), ("h", "main"), ("h", "main")]
SPLITS = ["N0", "N1", "N2", "Y0", "N3", "N4", "N5", "N6", "N7", "Y1", "N8"]
RESID_BEFORE = {0: 0, 2: 1, 3: 2, 4: 3, 5: 3, 7: 4, 8: 5}

HEADNORMS = ["mk0", "mq0", "k1", "mk1", "q1", "mq1"]
HEADTS = [("mk0", 0), ("mq0", 0), ("k1", 0), ("mk1", 0), ("q1", 0), ("q1", 1), ("q1", 2), ("mq1", 0)]

ROUNDS = [("mem", 0, 0, MEMH, 2), ("mem", 1, 0, MEMH, 2),
          ("band", 0, 0, NHA, 1), ("band", 1, 0, NHA // 2, 2), ("band", 1, NHA // 2, NHA // 2, 2),
          ("mem", 0, 0, MEMH, 2), ("mem", 1, 0, MEMH, 2)]
LAYER_ROUNDS = [(0, 2), (2, 7)]
SMALL_LOADS = 16
SOFT = 1536


def shape_constants():
    ident = np.eye(P, dtype=np.float32)
    t = np.arange(S)
    band = np.zeros((S, GROUPS, S), np.float32)
    inv_count = np.zeros((S, GROUPS), np.float32)
    for g, w in enumerate(WINDOWS):
        count = np.minimum(t + 1, w)
        inside = (t[:, None] <= t[None, :]) & (t[:, None] > t[None, :] - w)
        band[:, g, :] = inside.astype(np.float32)
        band[t, g, t] -= count.astype(np.float32)
        inv_count[:, g] = (1.0 / count).astype(np.float32)
    diff = t[:, None] // CHUNK - t[None, :] // CHUNK
    mask = np.where((diff >= 0) & (diff <= 1), 0.0, NEG_INF).astype(np.float32)
    expo = -np.arange(0, ROT, 2, dtype=np.float32) / np.float32(ROT)
    inv_freq = (500000.0 ** expo.astype(np.float64)).astype(np.float32)
    return {
        "c_ident": ident,
        "c_band0": np.ascontiguousarray(band[0:P]),
        "c_band1": np.ascontiguousarray(band[P:S, :, P:S]),
        "c_inv_count": np.ascontiguousarray(inv_count.reshape(NT, P, GROUPS).transpose(1, 0, 2)),
        "c_mask": np.ascontiguousarray(np.concatenate([mask[0:P, 0:P], mask[P:S]], axis=1)),
        "c_inv_freq": inv_freq,
    }


def encoder_kernel(nc, a, out):
    with ExitStack() as ctx:
        def sb(name, shape, dt=F32):
            return ctx.enter_context(nc.sbuf_tensor(name, shape, dt))

        def sem(name):
            return ctx.enter_context(nc.semaphore(name))

        ps = ctx.enter_context(nc.psum_tensor("ps", [P, 8, 512], F32))

        w_raw = [sb(f"w_raw{s}", [P, 4, 512]) for s in range(SLOTS)]
        w_hi = [sb(f"w_hi{s}", [P, 4, 512], F32R) for s in range(SLOTS)]
        w_lo = [sb(f"w_lo{s}", [P, 4, 512], F32R) for s in range(SLOTS)]
        h = sb("h", [P, NT, D])
        xn = sb("xn", [P, NT, D])
        ycat = sb("ycat", [P, NT, D])
        tr_hi = {n: sb(f"{n}T_hi", [P, KC, S], F32R) for n in ("main", "side")}
        tr_lo = {n: sb(f"{n}T_lo", [P, KC, S], F32R) for n in ("main", "side")}
        gain = sb("gain", [P, 2, D])
        silu_g = sb("silu_g", [P, NT, FB])
        act_f = sb("act_f", [P, NT, FB])
        actT_hi = sb("actT_hi", [P, 2, NT, P], F32R)
        actT_lo = sb("actT_lo", [P, 2, NT, P], F32R)
        kv_sb = sb("kv_sb", [P, NT, 512])
        mkv_sb = sb("mkv_sb", [P, NT, 512])
        kT = sb("kT", [HD, KVH, S])
        mkT = sb("mkT", [HD, MEMH, S])
        mqT = sb("mqT", [HD, MEMH, S])
        shared = sb("shared", [P, 3840])
        band0 = shared[:, 0:1024].rearrange("p (g t) -> p g t", g=GROUPS)
        band1 = shared[:, 1024:1536].rearrange("p (g t) -> p g t", g=GROUPS)
        pool_w = shared[0:GC, 1536:3072].rearrange("p (g c d) -> p g c d", g=GROUPS, c=2)
        pool_scale = shared[:, 3072:3840]
        qT = shared[0:HD, 0:NHA * S].rearrange("p (n t) -> p n t", n=NHA)
        probs = sb("probs", [P, 2, SOFT])
        pooledT = probs[0:GC, :, :].rearrange("p a b -> p (a b)")[:, 0:8 * S].rearrange("p (c t) -> p c t", c=8)
        pT = sb("pT", [P, SOFT])
        ident = sb("ident", [P, P])
        mask = sb("mask", [P, 3 * P])
        inv_count = sb("inv_count", [P, NT, GROUPS])
        head_gain = sb("head_gain", [P, 6, HD])
        sinks = sb("sinks", [P, NHA])
        pos_i = sb("pos_i", [P, NT], I32)
        inv_freq = sb("inv_freq", [P, RH])
        rope = sb("rope", [P, 8, NT, RH])
        rot = sb("rot", [P, 4, NT * NHA * RH])
        row_ss = sb("row_ss", [P, 2 * NT])
        row_rs = sb("row_rs", [P, 2 * NT])
        row_ms = sb("row_ms", [P, 2 * NT])
        head_ss = sb("head_ss", [P, NT * NHA])
        head_ms = sb("head_ms", [P, NT * NHA])
        head_rs = sb("head_rs", [P, NT * NHA])
        minus_half = sb("minus_half", [P, NT * NHA])
        row_max = sb("row_max", [P, 2, NHA])
        sink_p = sb("sink_p", [P, 2, NHA])
        den = sb("den", [P, 2, NHA])
        squares = sb("squares", [P, D], mybir.dt.bfloat16)

        x_landed = sem("x_landed")
        x1_landed = sem("x1_landed")
        mem_landed = sem("mem_landed")
        mem_again_landed = sem("mem_again_landed")
        consts_landed = sem("consts_landed")
        ident_landed = sem("ident_landed")
        gain_landed = [sem(f"gain_landed{s}") for s in range(2)]
        raw_landed = [sem(f"raw_landed{s}") for s in range(SLOTS)]
        hi_ready = [sem(f"hi_ready{s}") for s in range(SLOTS)]
        lo_ready = [sem(f"lo_ready{s}") for s in range(SLOTS)]
        weights_used = [sem(f"weights_used{s}") for s in range(SLOTS)]
        row_summed = sem("row_summed")
        row_scaled = sem("row_scaled")
        xn_ready = sem("xn_ready")
        turned = sem("turned")
        split_hi = sem("split_hi")
        split_lo = sem("split_lo")
        gu_done = sem("gu_done")
        silu_ready = sem("silu_ready")
        act_ready = sem("act_ready")
        act_turned = sem("act_turned")
        actT_hi_ready = sem("actT_hi_ready")
        actT_lo_ready = sem("actT_lo_ready")
        sum_done = sem("sum_done")
        h_ready = sem("h_ready")
        mkv_done = sem("mkv_done")
        mkv_ready = sem("mkv_ready")
        kv_done = sem("kv_done")
        kv_ready = sem("kv_ready")
        z_done = sem("z_done")
        z_ready = sem("z_ready")
        head_summed = sem("head_summed")
        head_scaled = sem("head_scaled")
        head_ready = sem("head_ready")
        head_turned = sem("head_turned")
        headT_ready = sem("headT_ready")
        pooled_done = sem("pooled_done")
        pooled_ready = sem("pooled_ready")
        pool_y_done = sem("pool_y_done")
        pool_y_ready = sem("pool_y_ready")
        score_done = sem("score_done")
        score_read = sem("score_read")
        shifted = sem("shifted")
        max_ready = sem("max_ready")
        probs_ready = sem("probs_ready")
        probs_turned = sem("probs_turned")
        pT_ready_a = sem("pT_ready_a")
        pT_ready_v = sem("pT_ready_v")
        o_done = sem("o_done")
        o_ready = sem("o_ready")
        angle_ready = sem("angle_ready")
        rope_ready = sem("rope_ready")
        half_ready = sem("half_ready")
        dve_step = sem("dve_step")
        pool_step = sem("pool_step")
        out_landed = sem("out_landed")

        def slot(u):
            return u % SLOTS

        def cycle(u):
            return u // SLOTS

        def product_done(eng, t, first_done, count, u):
            if t == 0:
                eng.wait_ge(first_done, count)
            else:
                eng.wait_ge(weights_used[slot(u)], cycle(u) + 1)

        sum_units = [UNIT["ffn0"] + FFN_UNITS - 1, UNIT["out0"] + 3, UNIT["ffn1"] + FFN_UNITS - 1,
                     UNIT["ffn2"] + FFN_UNITS - 1, UNIT["out1"] + 3, UNIT["ffn3"] + FFN_UNITS - 1]

        def act_share(n):
            return -(-n // 1024) * 512

        def half(w, b):
            return w[:, 2 * b:2 * b + 2, :]

        def split_index(name, t, b):
            return (SPLITS.index(name) * NT + t) * 2 + b

        def head_view(name):
            src = {"mk": mkv_sb[:, :, 0:MEMH * HD], "k": kv_sb[:, :, 0:KVH * HD],
                   "mq": xn[:, :, MIXER:D], "q": xn[:, :, 0:MIXER]}[name[:-1]]
            return src.rearrange("p t (n d) -> p t n d", d=HD)

        block = ctx.enter_context(nc.Block())

        @block.sync
        def _(sp):
            w_gu = {f"ffn{f}": a[n][l].rearrange("(k p) (j f) -> p k j f", p=P, j=2) for f, (n, l) in
                    enumerate((("ffn1_w_gate_up", 0), ("ffn2_w_gate_up", 0), ("ffn1_w_gate_up", 1), ("ffn2_w_gate_up", 1)))}
            w_dn = {f"ffn{f}": a[n][l].rearrange("(c p) d -> p c d", p=P) for f, (n, l) in
                    enumerate((("ffn1_w_down", 0), ("ffn2_w_down", 0), ("ffn1_w_down", 1), ("ffn2_w_down", 1)))}
            dense = {"mkv0": a["w_mem_kv"][0], "mkv1": a["w_mem_kv"][1], "kv": a["w_kv"], "z0": a["w_in"][0],
                     "z1": a["w_in"][1], "out0": a["w_out"][0], "out1": a["w_out"][1]}

            def load(u, c, halves):
                if not isinstance(c, int) or c > 0:
                    sp.wait_ge(lo_ready[slot(u)], c * 2)
                for dst, src in halves:
                    sp.dma_start(dst, src).then_inc(raw_landed[slot(u)], 16)

            def load_ffn(name, i, c):
                u = UNIT[name]
                for j in range(2):
                    load(u + j, cycle(u + j) + c,
                         [(w_raw[slot(u + j)][:, :, g * FB:(g + 1) * FB],
                           w_gu[name][:, 4 * j:4 * j + 4, g, bass.ds(i * FB, FB)]) for g in range(2)])
                load(u + 2, cycle(u + 2) + c,
                     [(half(w_raw[slot(u + 2)], b).rearrange("p n d -> p (n d)"),
                       w_dn[name][:, bass.ds(i * 2 + b, 1), :].rearrange("p c d -> p (c d)")) for b in range(2)])

            def ffn(name):
                load_ffn(name, 0, 0)
                with sp.Fori(1, STEPS) as i:
                    load_ffn(name, i, i)

            def projection(name):
                w = dense[name].rearrange("(k p) n -> p k n", p=P)
                for n in range(w.shape[2] // 512):
                    for j in range(2):
                        u = UNIT[name] + 2 * n + j
                        load(u, cycle(u), [(half(w_raw[slot(u)], b),
                                            w[:, 4 * j + 2 * b:4 * j + 2 * b + 2, n * 512:(n + 1) * 512]) for b in range(2)])

            x_dram = a["x"][0].rearrange("(t p) d -> p t d", p=P)
            sp.dma_start(h[:, 0, :], x_dram[:, 0, :]).then_inc(x_landed, 16)
            for name in ("ffn0", "mkv0", "z0", "out0", "ffn1", "kv", "ffn2", "mkv1", "z1", "out1", "ffn3"):
                if name.startswith("ffn"):
                    ffn(name)
                else:
                    projection(name)
            out_dram = out[0].rearrange("(t p) d -> p t d", p=P)
            for t in range(NT):
                sp.wait_ge(h_ready, 5 * NT + t + 1)
                sp.dma_start(out_dram[:, t, :], h[:, t, :]).then_inc(out_landed, 16)
            sp.wait_ge(out_landed, 16 * NT)

        gains = [a["ffn1_norm"][0], a["mem_norm"][0], a["mix_norm"][0], a["ffn2_norm"][0], a["kv_norm"],
                 a["ffn1_norm"][1], a["mem_norm"][1], a["mix_norm"][1], a["ffn2_norm"][1]]

        @block.gpsimd
        def _(pool):
            step = [0]

            def link(ins):
                step[0] += 1
                ins.then_inc(pool_step, 1)
                pool.wait_ge(pool_step, step[0])

            def load_gain(k):
                if k >= 2:
                    pool.wait_ge(xn_ready, (k - 2) * NT + NT)
                pool.dma_start(gain[:, k % 2, :], gains[k].partition_broadcast(P)).then_inc(gain_landed[k % 2], 16)

            def load_mem():
                pool.dma_start(ycat[:, :, :], a["mem"][0].rearrange("(t p) d -> p t d", p=P)).then_inc(mem_again_landed, 16)

            def row_roots(k):
                for t in range(NT):
                    c = (k % 2) * NT + t
                    pool.wait_ge(row_summed, k * NT + t + 1)
                    link(nc.gpsimd.tensor_scalar(row_ms[:, c:c + 1], row_ss[:, c:c + 1], 1.0 / D, EPS, ALU.mult, ALU.add))
                    nc.gpsimd.tensor_tensor(row_rs[:, c:c + 1], row_ms[:, c:c + 1], minus_half[:, 0:1],
                                            ALU.pow).then_inc(row_scaled, 1)

            def head_roots(name):
                x = HEADNORMS.index(name)
                n = head_view(name).shape[1] * head_view(name).shape[2]
                pool.wait_ge(head_summed, x + 1)
                link(nc.gpsimd.tensor_scalar(head_ms[:, 0:n], head_ss[:, 0:n], 1.0 / HD, EPS, ALU.mult, ALU.add))
                nc.gpsimd.tensor_tensor(head_rs[:, 0:n], head_ms[:, 0:n], minus_half[:, 0:n],
                                        ALU.pow).then_inc(head_scaled, 1)

            load_gain(0)
            pool.dma_start(ident[:, :], a["c_ident"]).then_inc(ident_landed, 16)
            link(nc.gpsimd.memset(minus_half[:, :], -0.5))
            row_roots(0)
            load_gain(1)
            small = [
                (inv_freq[:, :], a["c_inv_freq"].partition_broadcast(P)),
                (pos_i[:, 0:1], a["positions"][0, 0:P].rearrange("(p o) -> p o", o=1)),
                (pos_i[:, 1:2], a["positions"][0, P:S].rearrange("(p o) -> p o", o=1)),
                (band0, a["c_band0"]),
                (band1, a["c_band1"]),
                (inv_count[:, :, :], a["c_inv_count"]),
                (mask[:, :], a["c_mask"]),
                (pool_w, a["pool_w"][0].rearrange("g (c p) d -> p g c d", p=GC)),
                (pool_scale, a["pool_scale"][0].partition_broadcast(P)),
                (head_gain[:, 0, :], a["mem_k_norm"][0].partition_broadcast(P)),
                (head_gain[:, 1, :], a["mem_q_norm"][0].partition_broadcast(P)),
                (head_gain[:, 2, :], a["k_norm"].partition_broadcast(P)),
                (head_gain[:, 3, :], a["mem_k_norm"][1].partition_broadcast(P)),
                (head_gain[:, 4, :], a["attn_q_norm"][0].partition_broadcast(P)),
                (head_gain[:, 5, :], a["mem_q_norm"][1].partition_broadcast(P)),
                (sinks[:, :], a["attn_sinks"][0].partition_broadcast(P)),
            ]
            assert len(small) == SMALL_LOADS
            for dst, src in small:
                pool.dma_start(dst, src).then_inc(consts_landed, 16)
            row_roots(1)
            load_gain(2)
            row_roots(2)
            load_gain(3)
            head_roots("mk0")
            head_roots("mq0")
            pool.wait_ge(turned, split_index("Y0", 1, 1) + 1)
            load_mem()
            for k in (3, 4, 5, 6):
                row_roots(k)
                load_gain(k + 1)
            head_roots("k1")
            row_roots(7)
            load_gain(8)
            head_roots("mk1")
            head_roots("q1")
            head_roots("mq1")
            row_roots(8)

        @block.scalar
        def _(act):
            def high(u, c):
                s = slot(u)
                act.wait_ge(raw_landed[s], (c + 1) * 32)
                if not isinstance(c, int) or c > 0:
                    act.wait_ge(weights_used[s], c)
                for b in range(2):
                    nc.scalar.copy(half(w_hi[s], b), half(w_raw[s], b)).then_inc(hi_ready[s], 1)

            def high_u(u):
                if u < UNITS:
                    high(u, cycle(u))

            def row_sum(k, t):
                src = h if NORMS[k][0] == "h" else ycat
                c = (k % 2) * NT + t
                if k == 0:
                    act.wait_ge(x_landed if t == 0 else x1_landed, 16)
                elif NORMS[k][0] == "mem":
                    act.wait_ge(mem_landed if k == 1 else mem_again_landed, 16)
                else:
                    act.wait_ge(h_ready, (RESID_BEFORE[k] - 1) * NT + t + 1)
                if k >= 2:
                    act.wait_ge(row_scaled, (k - 2) * NT + t + 1)
                if 2 * k + t > 0:
                    act.wait_ge(row_summed, 2 * k + t)
                nc.scalar.activation(squares[:, :], src[:, t, :], ACT.Square,
                                     accum_out=row_ss[:, c:c + 1]).then_inc(row_summed, 1)

            def split(name, t, dest):
                for b in range(2):
                    q = split_index(name, t, b)
                    act.wait_ge(turned, q + 1)
                    nc.scalar.copy(tr_hi[dest][:, 4 * b:4 * b + 4, t * P:(t + 1) * P],
                                   ps[:, TR_BANK + b, :].rearrange("p (k t) -> p k t", k=4)).then_inc(split_hi, 1)

            def silu(c, t, u, used):
                if t == 0:
                    act.wait_ge(gu_done, c + 1)
                else:
                    act.wait_ge(weights_used[slot(u + 1)], used + 1)
                nc.scalar.activation(silu_g[:, t, :], ps[:, GU_BANK + t, 0:FB], ACT.Silu).then_inc(silu_ready, 1)

            def actT_high(c):
                act.wait_ge(act_turned, c + 1)
                nc.scalar.copy(actT_hi[:, :, :, :].rearrange("p c t n -> p (c t n)"),
                               ps[:, TR_BANK, :]).then_inc(actT_hi_ready, 1)

            def ffn(f):
                u = UNIT[f"ffn{f}"]
                c0 = f * STEPS

                def step(i, c, first=False):
                    if not first:
                        high(u + 2, c - 1 + cycle(u + 2))
                    silu(c0 + c, 0, u, None)
                    if not first:
                        actT_high(c0 + c - 1)
                    high(u, c + 1 + cycle(u))
                    silu(c0 + c, 1, u, cycle(u + 1) + c)
                    high(u + 1, c + 1 + cycle(u + 1))

                step(0, 0, first=True)
                with act.Fori(1, STEPS - 1) as i:
                    step(i, i)
                last = STEPS - 1
                high(u + 2, last - 1 + cycle(u + 2))
                silu(c0 + last, 0, u, None)
                actT_high(c0 + last - 1)
                high_u(u + FFN_UNITS)
                silu(c0 + last, 1, u, cycle(u + 1) + last)
                high_u(u + FFN_UNITS + 1)
                high(u + 2, last + cycle(u + 2))
                actT_high(c0 + last)

            def head_copy(y):
                name, part = HEADTS[y]
                dst = {"mk0": mkT, "mk1": mkT, "k1": kT, "mq0": mqT, "mq1": mqT}.get(name)
                dst = qT[:, 4 * part:4 * part + 4, :] if dst is None else dst[:, :, :]
                bank = TR_BANK if y % 2 == 0 else GU_BANK
                act.wait_ge(head_turned, y + 1)
                nc.scalar.copy(dst.rearrange("p n t -> p (n t)"),
                               ps[0:HD, bank:bank + 2, :].rearrange("p b n -> p (b n)")).then_inc(headT_ready, 1)

            def z_copy(l):
                for n in range(2):
                    for t in range(NT):
                        product_done(act, t, z_done, l * 2 + n + 1, UNIT[f"z{l}"] + 2 * n + 1)
                        nc.scalar.copy(xn[:, t, n * 512:(n + 1) * 512],
                                       ps[:, SUM_BANK + 2 * t + n, :]).then_inc(z_ready, 1)

            def exponentials(r):
                kind, t, h0, nh, kb = ROUNDS[r]
                if kind == "band":
                    act.wait_ge(max_ready, r + 1)
                    nc.scalar.activation(sink_p[:, r % 2, 0:nh], sink_p[:, r % 2, 0:nh], ACT.Exp)
                act.wait_ge(shifted, r + 1)
                p = probs[:, r % 2, 0:nh * kb * P]
                nc.scalar.activation(p, p, ACT.Exp).then_inc(probs_ready, 1)

            def probs_copy(r):
                n = act_share(ROUNDS[r][3] * ROUNDS[r][4] * P)
                act.wait_ge(probs_turned, r + 1)
                if r > 0:
                    act.wait_ge(o_done, r)
                nc.scalar.copy(pT[:, 0:n], ps[:, PT_BANK:PT_BANK + 3, :].rearrange("p b n -> p (b n)")[:, 0:n]
                               ).then_inc(pT_ready_a, 1)

            def attention(l):
                r0, r1 = LAYER_ROUNDS[l]
                for r in range(r0, r1 + 1):
                    if r < r1:
                        exponentials(r)
                    if r > r0:
                        probs_copy(r - 1)

            def proj_high(name, m):
                for j in range(m):
                    high_u(UNIT[name] + 2 + j)

            x_dram = a["x"][0].rearrange("(t p) d -> p t d", p=P)
            act.dma_start(h[:, 1, :], x_dram[:, 1, :]).then_inc(x1_landed, 16)
            act.dma_start(ycat[:, :, :], a["mem"][0].rearrange("(t p) d -> p t d", p=P)).then_inc(mem_landed, 16)
            row_sum(0, 0)
            row_sum(0, 1)
            high_u(0)
            split("N0", 0, "main")
            split("N0", 1, "main")
            high_u(1)
            row_sum(1, 0)
            row_sum(1, 1)
            split("N1", 0, "side")
            split("N1", 1, "side")
            act.wait_ge(angle_ready, 1)
            nc.scalar.activation(rope[:, 6, :, :], rope[:, 4, :, :], ACT.Sin)
            nc.scalar.activation(rope[:, 7, :, :], rope[:, 5, :, :], ACT.Sin).then_inc(rope_ready, 1)
            ffn(0)
            row_sum(2, 0)
            row_sum(2, 1)
            proj_high("mkv0", 2)
            split("N2", 0, "main")
            split("N2", 1, "main")
            high_u(UNIT["z0"] + 2)
            high_u(UNIT["z0"] + 3)
            head_copy(0)
            high_u(UNIT["z0"] + 4)
            high_u(UNIT["z0"] + 5)
            z_copy(0)
            head_copy(1)
            for c in range(4):
                act.wait_ge(pooled_done, c + 1)
                nc.scalar.copy(pooledT[:, 2 * c:2 * c + 2, :].rearrange("p c t -> p (c t)"),
                               ps[0:GC, SUM_BANK + c, :]).then_inc(pooled_ready, 1)
            attention(0)
            split("Y0", 0, "main")
            split("Y0", 1, "main")
            proj_high("out0", 4)
            row_sum(3, 0)
            row_sum(3, 1)
            split("N3", 0, "main")
            split("N3", 1, "main")
            ffn(1)
            row_sum(4, 0)
            row_sum(4, 1)
            row_sum(5, 0)
            row_sum(5, 1)
            row_sum(6, 0)
            row_sum(6, 1)
            split("N4", 0, "side")
            split("N4", 1, "side")
            split("N5", 0, "main")
            split("N5", 1, "main")
            proj_high("kv", 2)
            product_done(act, 1, None, None, UNIT["kv"] + 1)
            split("N6", 0, "side")
            split("N6", 1, "side")
            ffn(2)
            row_sum(7, 0)
            row_sum(7, 1)
            proj_high("mkv1", 2)
            split("N7", 0, "main")
            split("N7", 1, "main")
            proj_high("z1", 4)
            z_copy(1)
            for y in range(2, len(HEADTS)):
                head_copy(y)
            attention(1)
            split("Y1", 0, "main")
            split("Y1", 1, "main")
            proj_high("out1", 4)
            row_sum(8, 0)
            row_sum(8, 1)
            split("N8", 0, "main")
            split("N8", 1, "main")
            ffn(3)

        @block.vector
        def _(dve):
            step_count = [0]

            def link(ins):
                step_count[0] += 1
                ins.then_inc(dve_step, 1)
                dve.wait_ge(dve_step, step_count[0])

            def low(u, c):
                s = slot(u)
                for b in range(2):
                    dve.wait_ge(hi_ready[s], c * 2 + (b + 1))
                    nc.vector.tensor_tensor(half(w_lo[s], b), half(w_raw[s], b), half(w_hi[s], b).bitcast(F32),
                                            ALU.subtract).then_inc(lo_ready[s], 1)

            def low_u(u):
                if u < UNITS:
                    low(u, cycle(u))

            def norm_rows(k, t):
                src = h if NORMS[k][0] == "h" else ycat
                c = (k % 2) * NT + t
                name = f"N{k}"
                if t == 0:
                    dve.wait_ge(gain_landed[k % 2], 16 * (k // 2 + 1))
                dve.wait_ge(row_scaled, k * NT + t + 1)
                q = split_index(name, t, 0)
                if q >= 2 * NT:
                    dve.wait_ge(turned, q - 2 * NT + 2)
                nc.vector.scalar_tensor_tensor(out=xn[:, t, :], in0=src[:, t, :], scalar=row_rs[:, c:c + 1],
                                               in1=gain[:, k % 2, :], op0=ALU.mult, op1=ALU.mult).then_inc(xn_ready, 1)

            def split(name, t, dest):
                for b in range(2):
                    q = split_index(name, t, b)
                    hi = tr_hi[dest][:, 4 * b:4 * b + 4, t * P:(t + 1) * P]
                    lo = tr_lo[dest][:, 4 * b:4 * b + 4, t * P:(t + 1) * P]
                    dve.wait_ge(split_hi, q + 1)
                    nc.vector.tensor_tensor(lo, ps[:, TR_BANK + b, :].rearrange("p (k t) -> p k t", k=4),
                                            hi.bitcast(F32), ALU.subtract).then_inc(split_lo, 1)

            def gated(c, t, wait_turned):
                dve.wait_ge(silu_ready, c * 2 + (t + 1))
                if wait_turned:
                    dve.wait_ge(act_turned, c)
                nc.vector.tensor_tensor(act_f[:, t, :], ps[:, GU_BANK + t, FB:2 * FB], silu_g[:, t, :],
                                        ALU.mult).then_inc(act_ready, 1)

            def actT_low(c):
                dve.wait_ge(actT_hi_ready, c + 1)
                nc.vector.tensor_tensor(actT_lo[:, :, :, :].rearrange("p c t n -> p (c t n)"), ps[:, TR_BANK, :],
                                        actT_hi[:, :, :, :].rearrange("p c t n -> p (c t n)").bitcast(F32),
                                        ALU.subtract).then_inc(actT_lo_ready, 1)

            def ffn(f):
                u = UNIT[f"ffn{f}"]
                c0 = f * STEPS

                def step(c, first=False):
                    if not first:
                        low(u + 2, c - 1 + cycle(u + 2))
                    gated(c0 + c, 0, not first)
                    if not first:
                        actT_low(c0 + c - 1)
                    low(u, c + 1 + cycle(u))
                    gated(c0 + c, 1, False)
                    low(u + 1, c + 1 + cycle(u + 1))

                step(0, first=True)
                with dve.Fori(1, STEPS - 1) as i:
                    step(i)
                last = STEPS - 1
                low(u + 2, last - 1 + cycle(u + 2))
                gated(c0 + last, 0, True)
                actT_low(c0 + last - 1)
                low_u(u + FFN_UNITS)
                gated(c0 + last, 1, False)
                low_u(u + FFN_UNITS + 1)
                low(u + 2, last + cycle(u + 2))
                actT_low(c0 + last)

            def residual(r, weight):
                for t in range(NT):
                    product_done(dve, t, sum_done, r + 1, sum_units[r])
                    nc.vector.scalar_tensor_tensor(
                        out=h[:, t, :], in0=ps[:, SUM_BANK + 2 * t:SUM_BANK + 2 * t + 2, :].rearrange("p b n -> p (b n)"),
                        scalar=weight, in1=h[:, t, :], op0=ALU.mult, op1=ALU.add).then_inc(h_ready, 1)

            def proj_low(name, m):
                for j in range(m):
                    low_u(UNIT[name] + 2 + j)

            def kv_copy(dst, done, ready, base, name):
                for t in range(NT):
                    product_done(dve, t, done, base // NT + 1, UNIT[name] + 1)
                    nc.vector.tensor_copy(dst[:, t, :], ps[:, GU_BANK + t, :]).then_inc(ready, 1)
                dve.wait_ge(ready, base + NT)

            def head_norm(name):
                x = HEADNORMS.index(name)
                v = head_view(name)
                nt, nh = v.shape[1], v.shape[2]
                n = nt * nh
                sq = pT[:, 0:n * HD].rearrange("p (n d) -> p n d", d=HD)
                rs = head_rs[:, 0:n].rearrange("p (t n) -> p t n", t=nt).unsqueeze(3).to_broadcast([P, nt, nh, HD])
                g = head_gain[:, x, :].unsqueeze(1).unsqueeze(1).to_broadcast([P, nt, nh, HD])
                link(nc.vector.tensor_tensor(sq.rearrange("p (t n) d -> p t n d", t=nt), v, v, ALU.mult))
                nc.vector.tensor_reduce(head_ss[:, 0:n], sq, AX.X, ALU.add).then_inc(head_summed, 1)
                dve.wait_ge(head_scaled, x + 1)
                link(nc.vector.tensor_tensor(v, v, rs, ALU.mult))
                ins = nc.vector.tensor_tensor(v, v, g, ALU.mult)
                if name[:-1] in ("mk", "mq"):
                    ins.then_inc(head_ready, 1)
                    return
                link(ins)
                x1, x2 = v[:, :, :, 0:RH], v[:, :, :, RH:ROT]
                cos, sin = (rope[:, i, :, :].unsqueeze(2).to_broadcast([P, nt, nh, RH]) for i in (6, 7))
                tmp = [rot[:, i, 0:n * RH].rearrange("p (t n d) -> p t n d", t=nt, n=nh) for i in range(4)]
                nc.vector.tensor_tensor(tmp[0], x1, cos, ALU.mult)
                nc.vector.tensor_tensor(tmp[1], x2, sin, ALU.mult)
                nc.vector.tensor_tensor(tmp[2], x2, cos, ALU.mult)
                link(nc.vector.tensor_tensor(tmp[3], x1, sin, ALU.mult))
                link(nc.vector.tensor_tensor(x1, tmp[0], tmp[1], ALU.subtract))
                nc.vector.tensor_tensor(x2, tmp[2], tmp[3], ALU.add).then_inc(head_ready, 1)

            def rope_tables():
                dve.wait_ge(consts_landed, 16 * SMALL_LOADS)
                pos, ang, whole, part, to_cos, to_sin = (rope[:, i, :, :] for i in range(6))
                posf = pos.rearrange("p t d -> p (t d)")[:, 0:NT]
                q1, q2, q3 = two_pi_parts()
                link(nc.vector.tensor_copy(posf, pos_i[:, :]))
                link(nc.vector.tensor_tensor(ang, posf.unsqueeze(2).to_broadcast([P, NT, RH]),
                                             inv_freq[:, :].unsqueeze(1).to_broadcast([P, NT, RH]), ALU.mult))
                link(nc.vector.tensor_scalar(whole, ang, 1.0 / (4096 * 2 * np.pi), MAGIC, ALU.mult, ALU.add))
                link(nc.vector.tensor_scalar(whole, whole, -MAGIC, 4096.0, ALU.add, ALU.mult))

                def less(turns, q):
                    link(nc.vector.scalar_tensor_tensor(out=ang, in0=turns, scalar=-q, in1=ang, op0=ALU.mult, op1=ALU.add))

                less(whole, q1)
                less(whole, q2)
                link(nc.vector.tensor_scalar(part, ang, 1.0 / (2 * np.pi), MAGIC, ALU.mult, ALU.add))
                link(nc.vector.tensor_scalar(part, part, -MAGIC, None, ALU.add))
                less(part, q1)
                less(part, q2)
                less(whole, q3)
                less(part, q3)
                link(nc.vector.tensor_scalar(to_sin, ang, 3.1415925, -3.1415925, ALU.min, ALU.max))
                link(nc.vector.tensor_scalar(part, to_sin, -1.0, None, ALU.mult))
                link(nc.vector.tensor_tensor(to_cos, part, to_sin, ALU.min))
                nc.vector.tensor_scalar(to_cos, to_cos, float(np.pi / 2), None, ALU.add).then_inc(angle_ready, 1)

            def softmax_scores(r):
                kind, t, h0, nh, kb = ROUNDS[r]
                width = kb * P
                s = ps[:, 0:3, :].rearrange("p b n -> p (b n)")[:, 0:nh * width].rearrange("p (n k) -> p n k", n=nh)
                p = probs[:, r % 2, 0:nh * width].rearrange("p (n k) -> p n k", n=nh)
                dve.wait_ge(score_done, r + 1)
                if r >= 2:
                    dve.wait_ge(probs_turned, r - 1)
                if kind == "band":
                    m = (mask[:, 0:P] if t == 0 else mask[:, P:3 * P]).unsqueeze(1).to_broadcast([P, nh, width])
                    ins = nc.vector.scalar_tensor_tensor(out=p, in0=s, scalar=SM_SCALE, in1=m, op0=ALU.mult, op1=ALU.add)
                else:
                    ins = nc.vector.tensor_scalar(p, s, SM_SCALE, None, ALU.mult)
                ins.then_inc(score_read, 1)
                dve.wait_ge(score_read, r + 1)
                mx = row_max[:, r % 2, 0:nh]
                link(nc.vector.tensor_reduce(mx, p, AX.X, ALU.max))
                if kind == "band":
                    link(nc.vector.tensor_tensor(mx, mx, sinks[:, h0:h0 + nh], ALU.max))
                    nc.vector.tensor_tensor(sink_p[:, r % 2, 0:nh], sinks[:, h0:h0 + nh], mx,
                                            ALU.subtract).then_inc(max_ready, 1)
                else:
                    ins = nc.vector.tensor_copy(den[:, r % 2, 0:nh], mx)
                    ins.then_inc(max_ready, 1)
                nc.vector.tensor_tensor(p, p, mx.unsqueeze(2).to_broadcast([P, nh, width]),
                                        ALU.subtract).then_inc(shifted, 1)

            def softmax_sum(r):
                kind, t, h0, nh, kb = ROUNDS[r]
                p = probs[:, r % 2, 0:nh * kb * P].rearrange("p (n k) -> p n k", n=nh)
                dn = den[:, r % 2, 0:nh]
                dve.wait_ge(probs_ready, r + 1)
                dve.wait_ge(max_ready, r + 1)
                link(nc.vector.tensor_reduce(dn, p, AX.X, ALU.add))
                if kind == "band":
                    link(nc.vector.tensor_tensor(dn, dn, sink_p[:, r % 2, 0:nh], ALU.add))
                link(nc.vector.reciprocal(dn, dn))
                n = act_share(nh * kb * P)
                dve.wait_ge(probs_turned, r + 1)
                if r > 0:
                    dve.wait_ge(o_done, r)
                nc.vector.tensor_copy(pT[:, n:nh * kb * P],
                                      ps[:, PT_BANK:PT_BANK + 3, :].rearrange("p b n -> p (b n)")[:, n:nh * kb * P]
                                      ).then_inc(pT_ready_v, 1)

            def output(r):
                kind, t, h0, nh, kb = ROUNDS[r]
                base = h0 * HD + (MIXER if kind == "mem" else 0)
                dve.wait_ge(o_done, r + 1)
                nc.vector.tensor_tensor(
                    ycat[:, t, base:base + nh * HD].rearrange("p (n d) -> p n d", d=HD),
                    ps[:, O_BANK:O_BANK + 2, :].rearrange("p b n -> p (b n)")[:, 0:nh * HD].rearrange("p (n d) -> p n d", d=HD),
                    den[:, r % 2, 0:nh].unsqueeze(2).to_broadcast([P, nh, HD]), ALU.mult).then_inc(o_ready, 1)

            def attention(l):
                r0, r1 = LAYER_ROUNDS[l]
                for r in range(r0, r1 + 1):
                    if r < r1:
                        softmax_scores(r)
                    if r > r0:
                        softmax_sum(r - 1)
                        output(r - 1)

            norm_rows(0, 0)
            norm_rows(0, 1)
            low_u(0)
            split("N0", 0, "main")
            split("N0", 1, "main")
            low_u(1)
            norm_rows(1, 0)
            norm_rows(1, 1)
            split("N1", 0, "side")
            split("N1", 1, "side")
            rope_tables()
            ffn(0)
            residual(0, 0.5)
            norm_rows(2, 0)
            norm_rows(2, 1)
            proj_low("mkv0", 2)
            kv_copy(mkv_sb, mkv_done, mkv_ready, 0, "mkv0")
            split("N2", 0, "main")
            split("N2", 1, "main")
            head_norm("mk0")
            proj_low("z0", 4)
            dve.wait_ge(z_ready, 2 * NT)
            head_norm("mq0")
            for t in range(NT):
                for g in range(GROUPS):
                    dve.wait_ge(pool_y_done, t + 1)
                    nc.vector.scalar_tensor_tensor(
                        out=ycat[:, t, g * GW:(g + 1) * GW],
                        in0=ps[:, SUM_BANK + 2 * t + g // 2, (g % 2) * GW:(g % 2 + 1) * GW],
                        scalar=inv_count[:, t, g:g + 1], in1=pool_scale[:, g * GW:(g + 1) * GW],
                        op0=ALU.mult, op1=ALU.mult).then_inc(pool_y_ready, 1)
            attention(0)
            split("Y0", 0, "main")
            split("Y0", 1, "main")
            proj_low("out0", 4)
            residual(1, 1.0)
            norm_rows(3, 0)
            norm_rows(3, 1)
            split("N3", 0, "main")
            split("N3", 1, "main")
            ffn(1)
            residual(2, 0.5)
            norm_rows(4, 0)
            norm_rows(4, 1)
            split("N4", 0, "side")
            norm_rows(5, 0)
            split("N4", 1, "side")
            norm_rows(5, 1)
            split("N5", 0, "main")
            norm_rows(6, 0)
            split("N5", 1, "main")
            norm_rows(6, 1)
            proj_low("kv", 2)
            kv_copy(kv_sb, kv_done, kv_ready, 0, "kv")
            split("N6", 0, "side")
            split("N6", 1, "side")
            ffn(2)
            residual(3, 0.5)
            dve.wait_ge(rope_ready, 1)
            head_norm("k1")
            norm_rows(7, 0)
            norm_rows(7, 1)
            proj_low("mkv1", 2)
            kv_copy(mkv_sb, mkv_done, mkv_ready, NT, "mkv1")
            split("N7", 0, "main")
            split("N7", 1, "main")
            head_norm("mk1")
            proj_low("z1", 4)
            dve.wait_ge(z_ready, 4 * NT)
            head_norm("q1")
            head_norm("mq1")
            attention(1)
            split("Y1", 0, "main")
            split("Y1", 1, "main")
            proj_low("out1", 4)
            residual(4, 1.0)
            norm_rows(8, 0)
            norm_rows(8, 1)
            split("N8", 0, "main")
            split("N8", 1, "main")
            ffn(3)
            residual(5, 0.5)

        @block.tensor
        def _(pe):
            def turn(name, src, ready, value):
                for t in range(NT):
                    pe.wait_ge(ready, value(t))
                    for b in range(2):
                        q = split_index(name, t, b)
                        if q >= 2:
                            pe.wait_ge(split_lo, q - 1)
                        for k in range(4):
                            c = (4 * b + k) * P
                            mm = pe.transpose(ps[:, TR_BANK + b, k * P:(k + 1) * P], src[:, t, c:c + P], ident[:, :])
                        mm.then_inc(turned, 1)

            def turn_norm(k):
                turn(f"N{k}", xn, xn_ready, lambda t: k * NT + t + 1)

            def three(dst, x_hi, x_lo, wh, wl, start, stop):
                pe.matmul(dst, x_hi, wh, start=start, stop=False)
                pe.matmul(dst, x_hi, wl, start=False, stop=False)
                return pe.matmul(dst, x_lo, wh, start=False, stop=stop)

            def product(u, c, t, dst, src, split_name, wait_src):
                for k in range(KC):
                    s = slot(u + k // 4)
                    kk = k % 4
                    if wait_src and k % 4 == 0:
                        pe.wait_ge(split_lo, split_index(split_name, t, k // 4) + 1)
                    if t == 0 and kk % 2 == 0:
                        pe.wait_ge(lo_ready[s], c[k // 4] * 2 + (kk // 2 + 1))
                    mm = three(dst, tr_hi[src][:, k, t * P:(t + 1) * P], tr_lo[src][:, k, t * P:(t + 1) * P],
                               w_hi[s][:, kk, :], w_lo[s][:, kk, :], k == 0, k == KC - 1)
                    if t == NT - 1 and kk == 3:
                        if k == KC - 1:
                            return mm, s
                        mm.then_inc(weights_used[s], 1)
                return mm, None

            def projection(name, src, split_name, bank, done, order):
                n_blocks = {"z0": 2, "z1": 2, "out0": 2, "out1": 2}.get(name, 1)
                for n in range(n_blocks):
                    for t in range(NT):
                        u = UNIT[name] + 2 * n
                        mm, s = product(u, (cycle(u), cycle(u + 1)), t, ps[:, bank(t, n), :], src, split_name, n == 0)
                        if s is not None:
                            mm.then_inc(weights_used[s], 1)
                        elif order(n):
                            mm.then_inc(done, 1)

            def ffn(f, split_name):
                u = UNIT[f"ffn{f}"]
                c0 = f * STEPS

                def gate_up(c, t, first=False):
                    if not first or f > 0:
                        pe.wait_ge(act_ready, (c0 + c) * 2 + (t - 1))
                    mm, s = product(u, (cycle(u) + c, cycle(u + 1) + c), t, ps[:, GU_BANK + t, :], "main", split_name, first)
                    mm.then_inc(gu_done if s is None else weights_used[s], 1)

                def turn_act(c):
                    pe.wait_ge(act_ready, (c0 + c) * 2 + 2)
                    for fc in range(2):
                        for t in range(NT):
                            mm = pe.transpose(ps[:, TR_BANK, (fc * NT + t) * P:(fc * NT + t + 1) * P],
                                              act_f[:, t, fc * P:(fc + 1) * P], ident[:, :])
                    mm.then_inc(act_turned, 1)

                def down(c, first=False, last=False):
                    s = slot(u + 2)
                    pe.wait_ge(actT_lo_ready, c0 + c + 1)
                    for t in range(NT):
                        for fc in range(2):
                            if t == 0:
                                pe.wait_ge(lo_ready[s], (cycle(u + 2) + c) * 2 + (fc + 1))
                            xh, xl = actT_hi[:, fc, t, :], actT_lo[:, fc, t, :]
                            wh = [w_hi[s][:, 2 * fc + n, :] for n in range(2)]
                            wl = [w_lo[s][:, 2 * fc + n, :] for n in range(2)]
                            dst = [ps[:, SUM_BANK + 2 * t + n, :] for n in range(2)]
                            for n in range(2):
                                pe.matmul(dst[n], xh, wh[n], start=first and fc == 0, stop=False)
                            for n in range(2):
                                pe.matmul(dst[n], xh, wl[n], start=False, stop=False)
                            for n in range(2):
                                mm = pe.matmul(dst[n], xl, wh[n], start=False, stop=last and fc == 1)
                        if t == NT - 1:
                            mm.then_inc(weights_used[s], 1)
                        elif last:
                            mm.then_inc(sum_done, 1)

                gate_up(0, 0, first=True)
                gate_up(0, 1, first=True)
                gate_up(1, 0)
                turn_act(0)
                gate_up(1, 1)
                down(0, first=True)
                with pe.Fori(2, STEPS) as i:
                    gate_up(i, 0)
                    turn_act(i - 1)
                    gate_up(i, 1)
                    down(i - 1)
                turn_act(STEPS - 1)
                down(STEPS - 1, last=True)

            def turn_heads(y):
                name, part = HEADTS[y]
                v = head_view(name)
                bank = TR_BANK if y % 2 == 0 else GU_BANK
                pe.wait_ge(head_ready, HEADNORMS.index(name) + 1)
                if y >= 2:
                    pe.wait_ge(headT_ready, y - 1)
                dst = ps[0:HD, bank:bank + 2, :].rearrange("p b (n t k) -> p (b n) t k", n=2, t=NT)
                for n in range(4):
                    for t in range(NT):
                        mm = pe.transpose(dst[:, n, t, :], v[:, t, 4 * part + n, :], ident[:, :])
                mm.then_inc(head_turned, 1)

            def scores(r):
                kind, t, h0, nh, kb = ROUNDS[r]
                flat = ps[:, 0:3, :].rearrange("p b n -> p (b n)")
                width = kb * P
                if r > 0:
                    pe.wait_ge(score_read, r)
                for n in range(nh):
                    q, k = (mqT[:, n, :], mkT[:, n, :]) if kind == "mem" else (qT[:, h0 + n, :], kT[:, (h0 + n) // GQA, :])
                    mm = pe.matmul(flat[:, n * width:(n + 1) * width], q[:, t * P:(t + 1) * P], k[:, 0:width],
                                   start=True, stop=True)
                mm.then_inc(score_done, 1)

            def turn_probs(r):
                kind, t, h0, nh, kb = ROUNDS[r]
                flat = ps[:, PT_BANK:PT_BANK + 3, :].rearrange("p b n -> p (b n)")
                pe.wait_ge(probs_ready, r + 1)
                if r > 0:
                    pe.wait_ge(pT_ready_a, r)
                    pe.wait_ge(pT_ready_v, r)
                for n in range(nh * kb):
                    mm = pe.transpose(flat[:, n * P:(n + 1) * P], probs[:, r % 2, n * P:(n + 1) * P], ident[:, :])
                mm.then_inc(probs_turned, 1)

            def values(r):
                kind, t, h0, nh, kb = ROUNDS[r]
                flat = ps[:, O_BANK:O_BANK + 2, :].rearrange("p b n -> p (b n)")
                pe.wait_ge(pT_ready_a, r + 1)
                pe.wait_ge(pT_ready_v, r + 1)
                if r > 0:
                    pe.wait_ge(o_ready, r)
                for n in range(nh):
                    kv = n if kind == "mem" else (h0 + n) // GQA
                    v = (mkv_sb if kind == "mem" else kv_sb)[:, :, 256 + kv * HD:256 + (kv + 1) * HD]
                    for b in range(kb):
                        j = n * kb + b
                        mm = pe.matmul(flat[:, n * HD:(n + 1) * HD], pT[:, j * P:(j + 1) * P], v[:, b, :],
                                       start=(b == 0), stop=(b == kb - 1))
                mm.then_inc(o_done, 1)

            def attention(l):
                r0, r1 = LAYER_ROUNDS[l]
                for r in range(r0, r1 + 1):
                    if r < r1:
                        scores(r)
                    if r > r0:
                        turn_probs(r - 1)
                        values(r - 1)

            def pooling():
                pe.wait_ge(z_ready, 2 * NT)
                for c in range(8):
                    dst = ps[0:GC, SUM_BANK + c // 2, (c % 2) * S:(c % 2 + 1) * S]
                    cols = slice(c * GC, (c + 1) * GC)
                    pe.matmul(dst, xn[:, 0, cols], band0[:, c // 2, :], start=True, stop=False)
                    mm = pe.matmul(dst[:, P:S], xn[:, 1, cols], band1[:, c // 2, :], start=False, stop=True)
                    if c % 2 == 1:
                        mm.then_inc(pooled_done, 1)
                pe.wait_ge(pooled_ready, 4)
                for t in range(NT):
                    for g in range(GROUPS):
                        dst = ps[:, SUM_BANK + 2 * t + g // 2, (g % 2) * GW:(g % 2 + 1) * GW]
                        for c in range(2):
                            mm = pe.matmul(dst, pooledT[:, 2 * g + c, t * P:(t + 1) * P], pool_w[:, g, c, :],
                                           start=(c == 0), stop=(c == 1))
                    mm.then_inc(pool_y_done, 1)

            def to_gu(t, n):
                return GU_BANK + t

            def to_sum(t, n):
                return SUM_BANK + 2 * t + n

            pe.wait_ge(ident_landed, 16)
            turn_norm(0)
            turn_norm(1)
            ffn(0, "N0")
            projection("mkv0", "side", "N1", to_gu, mkv_done, lambda n: True)
            turn_norm(2)
            pe.wait_ge(h_ready, NT)
            projection("z0", "main", "N2", to_sum, z_done, lambda n: True)
            pe.wait_ge(mkv_ready, NT)
            turn_heads(0)
            pe.wait_ge(consts_landed, 16 * SMALL_LOADS)
            turn_heads(1)
            pooling()
            pe.wait_ge(headT_ready, 2)
            pe.wait_ge(pool_y_ready, NT * GROUPS)
            attention(0)
            turn("Y0", ycat, o_ready, lambda t: LAYER_ROUNDS[0][1])
            projection("out0", "main", "Y0", to_sum, sum_done, lambda n: n == 1)
            turn_norm(3)
            ffn(1, "N3")
            turn_norm(4)
            turn_norm(5)
            projection("kv", "side", "N4", to_gu, kv_done, lambda n: True)
            turn_norm(6)
            pe.wait_ge(kv_ready, NT)
            ffn(2, "N5")
            projection("mkv1", "side", "N6", to_gu, mkv_done, lambda n: True)
            turn_norm(7)
            pe.wait_ge(h_ready, 4 * NT)
            projection("z1", "main", "N7", to_sum, z_done, lambda n: True)
            pe.wait_ge(mkv_ready, 2 * NT)
            for y in range(2, len(HEADTS)):
                turn_heads(y)
            pe.wait_ge(headT_ready, len(HEADTS))
            attention(1)
            turn("Y1", ycat, o_ready, lambda t: LAYER_ROUNDS[1][1])
            projection("out1", "main", "Y1", to_sum, sum_done, lambda n: n == 1)
            turn_norm(8)
            ffn(3, "N8")


_INS = ['x', 'mem', 'positions', 'ffn1_norm', 'ffn1_w_gate_up', 'ffn1_w_down', 'mix_norm', 'w_in', 'w_out',
        'pool_w', 'pool_scale', 'attn_q_norm', 'attn_sinks', 'kv_norm', 'w_kv', 'k_norm',
        'mem_norm', 'w_mem_kv', 'mem_q_norm', 'mem_k_norm', 'ffn2_norm', 'ffn2_w_gate_up', 'ffn2_w_down']


def kernel(**inputs):
    import numpy as _np
    import concourse.bacc as _bacc
    from concourse import mybir as _mybir
    from concourse.bass_utils import run_bass_kernel_spmd as _run

    nc = _bacc.Bacc("TRN2", target_bir_lowering=False, num_devices=1)
    arrays, aps = {}, {}
    for name, value in [(n, inputs[n]) for n in _INS] + list(shape_constants().items()):
        v = _np.ascontiguousarray(value)
        arrays[f"in_{name}_dram"] = v
        aps[name] = nc.dram_tensor(f"in_{name}_dram", v.shape, _mybir.dt.from_np(v.dtype), kind="ExternalInput").ap()
    out = nc.dram_tensor("out_0_dram", (1, S, D), _mybir.dt.float32, kind="ExternalOutput").ap()
    encoder_kernel(nc, aps, out)
    r = _run(nc, [arrays], core_ids=[0])
    return r.results[0]["out_0_dram"]
```

```python
from contextlib import ExitStack

import numpy as np

import concourse.bass as bass
from concourse import mybir

F32 = mybir.dt.float32
F32R = mybir.dt.float32r
I32 = mybir.dt.int32
ALU = mybir.AluOpType
ACT = mybir.ActivationFunctionType
AX = mybir.AxisListType

P = 128
D = 1024
S = 256
NT = S // P
KC = D // P
FF = ((8 * D // 3 + 127) // 128) * 128
FB = 256
STEPS = FF // FB
HD = 64
MIXER = 768
NHA = MIXER // HD
KVH = 4
GQA = NHA // KVH
MEMH = 4
GROUPS = 4
GW = MIXER // GROUPS
GC = GW // 2
WINDOWS = (2, 4, 8, 16)
CHUNK = 64
ROT = HD // 4
RH = ROT // 2
EPS = 1e-6
NEG_INF = -1e30
SM_SCALE = HD ** -0.5
SLOTS = 3
MAGIC = 1.5 * 2.0 ** 23

SUM_BANK = 0
GU_BANK = 4
TR_BANK = 6
PT_BANK = 4
O_BANK = 6


def two_pi_parts():
    a = np.floor(2 * np.pi * 2 ** 9) / 2 ** 9
    b = np.floor((2 * np.pi - a) * 2 ** 22) / 2 ** 22
    return float(a), float(b), float(2 * np.pi - a - b)


FFN_UNITS = 3 * STEPS
UNIT = {}
_u = 0
for _name, _n in (("ffn0", FFN_UNITS), ("mkv0", 2), ("z0", 4), ("out0", 4), ("ffn1", FFN_UNITS), ("kv", 2),
                  ("ffn2", FFN_UNITS), ("mkv1", 2), ("z1", 4), ("out1", 4), ("ffn3", FFN_UNITS)):
    UNIT[_name] = _u
    _u += _n
UNITS = _u
STAGES = list(UNIT)

NORMS = [("h", "main"), ("mem", "side"), ("h", "main"), ("h", "main"), ("h", "side"), ("h", "main"),
         ("mem", "side"), ("h", "main"), ("h", "main")]
SPLITS = ["N0", "N1", "N2", "Y0", "N3", "N4", "N5", "N6", "N7", "Y1", "N8"]
RESID_BEFORE = {0: 0, 2: 1, 3: 2, 4: 3, 5: 3, 7: 4, 8: 5}

HEADNORMS = ["mk0", "mq0", "k1", "mk1", "qa1", "qm1"]
HEADTS = [("mk0", 0, 6, 0), ("mq0", 0, 0, 1), ("k1", 0, 6, 2), ("mk1", 0, 4, 3),
          ("qa1", 0, 6, 4), ("qa1", 1, 4, 4), ("qm1", 0, 6, 4), ("qm1", 1, 4, 5)]

ROUNDS = [("mem", 0, 0, MEMH, 2 * P), ("mem", 1, 0, MEMH, 2 * P),
          ("band", 0, 0, 8, P), ("band", 1, 0, 8, P), ("band", 0, 8, 4, P), ("band", 1, 8, 4, P),
          ("mem", 0, 0, MEMH, 2 * P), ("mem", 1, 0, MEMH, 2 * P)]
LAYER_ROUNDS = [(0, 2), (2, 8)]
SMALL_LOADS = 18
SOFT = 1024


def shape_constants():
    ident = np.eye(P, dtype=np.float32)
    t = np.arange(S)
    band = np.zeros((S, GROUPS, S), np.float32)
    inv_count = np.zeros((S, GROUPS), np.float32)
    for g, w in enumerate(WINDOWS):
        count = np.minimum(t + 1, w)
        inside = (t[:, None] <= t[None, :]) & (t[:, None] > t[None, :] - w)
        band[:, g, :] = inside.astype(np.float32)
        band[t, g, t] -= count.astype(np.float32)
        inv_count[:, g] = (1.0 / count).astype(np.float32)
    mask = np.where(t[:P, None] // CHUNK >= t[None, :P] // CHUNK, 0.0, NEG_INF).astype(np.float32)
    expo = -np.arange(0, ROT, 2, dtype=np.float32) / np.float32(ROT)
    inv_freq = (500000.0 ** expo.astype(np.float64)).astype(np.float32)
    return {
        "c_ident": ident,
        "c_band0": np.ascontiguousarray(band[0:P]),
        "c_band1": np.ascontiguousarray(band[P:S, :, P:S]),
        "c_inv_count": np.ascontiguousarray(inv_count.reshape(NT, P, GROUPS).transpose(1, 0, 2)),
        "c_mask": mask,
        "c_inv_freq": inv_freq,
    }


def encoder_kernel(nc, a, out):
    with ExitStack() as ctx:
        def sb(name, shape, dt=F32):
            return ctx.enter_context(nc.sbuf_tensor(name, shape, dt))

        def sem(name):
            return ctx.enter_context(nc.semaphore(name))

        ps = ctx.enter_context(nc.psum_tensor("ps", [P, 8, 512], F32))

        w_raw = [sb(f"w_raw{s}", [P, 4, 512]) for s in range(SLOTS)]
        w_hi = [sb(f"w_hi{s}", [P, 4, 512], F32R) for s in range(SLOTS)]
        w_lo = [sb(f"w_lo{s}", [P, 4, 512], F32R) for s in range(SLOTS)]
        h = sb("h", [P, NT, D])
        xn = sb("xn", [P, NT, D])
        ycat = sb("ycat", [P, NT, D])
        tr_hi = {n: sb(f"{n}T_hi", [P, KC, S], F32R) for n in ("main", "side")}
        tr_lo = {n: sb(f"{n}T_lo", [P, KC, S], F32R) for n in ("main", "side")}
        gain = sb("gain", [P, 2, D])
        silu_g = sb("silu_g", [P, NT, FB])
        act_f = sb("act_f", [P, NT, FB])
        actT_hi = sb("actT_hi", [P, 2, NT, P], F32R)
        actT_lo = sb("actT_lo", [P, 2, NT, P], F32R)
        kv_sb = sb("kv_sb", [P, NT, 512])
        mkv_sb = sb("mkv_sb", [P, NT, 512])
        kT = sb("kT", [HD, KVH, S])
        mkT = sb("mkT", [HD, MEMH, S])
        mqT = sb("mqT", [HD, MEMH, S])
        shared = sb("shared", [P, 3840])
        band0 = shared[:, 0:1024].rearrange("p (g t) -> p g t", g=GROUPS)
        band1 = shared[:, 1024:1536].rearrange("p (g t) -> p g t", g=GROUPS)
        pool_w = shared[0:GC, 1536:3072].rearrange("p (g c d) -> p g c d", g=GROUPS, c=2)
        pool_scale = shared[:, 3072:3840]
        qT = shared[0:HD, 0:NHA * S].rearrange("p (n t) -> p n t", n=NHA)
        probs = sb("probs", [P, 2, SOFT])
        pooledT = probs[0:GC, :, :].rearrange("p a b -> p (a b)")[:, 0:8 * S].rearrange("p (c t) -> p c t", c=8)
        pT = sb("pT", [P, SOFT])
        ident = sb("ident", [P, P])
        mask = sb("mask", [P, P])
        v_mixed = sb("v_mixed", [P, KVH * HD])
        head_gain_col = sb("head_gain_col", [HD, 6])
        inv_count = sb("inv_count", [P, NT, GROUPS])
        rot_gain = sb("rot_gain", [P, 2, ROT])
        sinks = sb("sinks", [P, NHA])
        pos_i = sb("pos_i", [P, NT], I32)
        inv_freq = sb("inv_freq", [P, RH])
        rope = sb("rope", [P, 8, NT, RH])
        rot = sb("rot", [P, 4, NT * NHA * RH])
        row_ss = sb("row_ss", [P, 2 * NT])
        row_rs = sb("row_rs", [P, 2 * NT])
        row_ms = sb("row_ms", [P, 2 * NT])
        head_ss = sb("head_ss", [P, NT * NHA])
        head_ms = sb("head_ms", [P, NT * NHA])
        head_rs = sb("head_rs", [P, NT * NHA])
        minus_half = sb("minus_half", [P, NT * NHA])
        row_max = sb("row_max", [P, 2, 8])
        neg_max = sb("neg_max", [P, 2, 8])
        sink_p = sb("sink_p", [P, 2, 8])
        den = sb("den", [P, 2, 8])
        squares = sb("squares", [P, D], mybir.dt.bfloat16)

        x_landed = sem("x_landed")
        x1_landed = sem("x1_landed")
        mem_landed = sem("mem_landed")
        mem_again_landed = sem("mem_again_landed")
        consts_landed = sem("consts_landed")
        ident_landed = sem("ident_landed")
        gain_landed = [sem(f"gain_landed{s}") for s in range(2)]
        raw_landed = [sem(f"raw_landed{s}") for s in range(SLOTS)]
        hi_ready = [sem(f"hi_ready{s}") for s in range(SLOTS)]
        lo_ready = [sem(f"lo_ready{s}") for s in range(SLOTS)]
        weights_used = [sem(f"weights_used{s}") for s in range(SLOTS)]
        row_summed = sem("row_summed")
        row_scaled = sem("row_scaled")
        xn_ready = sem("xn_ready")
        turned = sem("turned")
        split_hi = sem("split_hi")
        split_lo = sem("split_lo")
        gu_done = sem("gu_done")
        silu_ready = sem("silu_ready")
        act_ready = sem("act_ready")
        act_turned = sem("act_turned")
        actT_hi_ready = sem("actT_hi_ready")
        actT_lo_ready = sem("actT_lo_ready")
        sum_done = sem("sum_done")
        h_ready = sem("h_ready")
        mkv_done = sem("mkv_done")
        mkv_ready = sem("mkv_ready")
        kv_done = sem("kv_done")
        kv_ready = sem("kv_ready")
        mixed_ready = sem("mixed_ready")
        ones_ready = sem("ones_ready")
        z_done = sem("z_done")
        z_ready = sem("z_ready")
        head_summed = sem("head_summed")
        head_scaled = sem("head_scaled")
        head_ready = sem("head_ready")
        head_turned = sem("head_turned")
        headT_ready = sem("headT_ready")
        pooled_done = sem("pooled_done")
        pooled_ready = sem("pooled_ready")
        pool_y_done = sem("pool_y_done")
        pool_y_ready = sem("pool_y_ready")
        score_done = sem("score_done")
        max_ready = sem("max_ready")
        probs_ready = sem("probs_ready")
        probs_turned = sem("probs_turned")
        pT_ready = sem("pT_ready")
        o_done = sem("o_done")
        o_ready = sem("o_ready")
        angle_ready = sem("angle_ready")
        rope_ready = sem("rope_ready")
        half_ready = sem("half_ready")
        dve_step = sem("dve_step")
        pool_step = sem("pool_step")
        out_landed = sem("out_landed")

        def slot(u):
            return u % SLOTS

        def cycle(u):
            return u // SLOTS

        def product_done(eng, t, first_done, count, u):
            if t == 0:
                eng.wait_ge(first_done, count)
            else:
                eng.wait_ge(weights_used[slot(u)], cycle(u) * 2 + 2)

        sum_units = [UNIT["ffn0"] + FFN_UNITS - 1, UNIT["out0"] + 3, UNIT["ffn1"] + FFN_UNITS - 1,
                     UNIT["ffn2"] + FFN_UNITS - 1, UNIT["out1"] + 3, UNIT["ffn3"] + FFN_UNITS - 1]

        def half(w, b):
            return w[:, 2 * b:2 * b + 2, :]

        def split_index(name, t, b):
            return (SPLITS.index(name) * NT + t) * 2 + b

        def head_view(name):
            src = {"mk": mkv_sb[:, :, 0:MEMH * HD], "k": kv_sb[:, :, 0:KVH * HD],
                   "mq": xn[:, :, MIXER:D], "qa": xn[:, :, 0:8 * HD], "qm": xn[:, :, 8 * HD:D]}[name[:-1]]
            return src.rearrange("p t (n d) -> p t n d", d=HD)

        def score_view(r):
            kind, t, h0, nh, width = ROUNDS[r]
            flat = ps[:, 2 * (r % 2):2 * (r % 2) + 2, :].rearrange("p b n -> p (b n)")
            return flat[:, 0:nh * width].rearrange("p (n k) -> p n k", n=nh)

        def probs_view(r):
            kind, t, h0, nh, width = ROUNDS[r]
            return probs[:, r % 2, 0:nh * width].rearrange("p (n k) -> p n k", n=nh)

        block = ctx.enter_context(nc.Block())

        @block.sync
        def _(sp):
            w_gu = {f"ffn{f}": a[n][l].rearrange("(k p) (j f) -> p k j f", p=P, j=2) for f, (n, l) in
                    enumerate((("ffn1_w_gate_up", 0), ("ffn2_w_gate_up", 0), ("ffn1_w_gate_up", 1), ("ffn2_w_gate_up", 1)))}
            w_dn = {f"ffn{f}": a[n][l].rearrange("(c p) d -> p c d", p=P) for f, (n, l) in
                    enumerate((("ffn1_w_down", 0), ("ffn2_w_down", 0), ("ffn1_w_down", 1), ("ffn2_w_down", 1)))}
            dense = {"mkv0": a["w_mem_kv"][0], "mkv1": a["w_mem_kv"][1], "kv": a["w_kv"], "z0": a["w_in"][0],
                     "z1": a["w_in"][1], "out0": a["w_out"][0], "out1": a["w_out"][1]}

            def load(u, c, halves):
                if not isinstance(c, int) or c > 0:
                    sp.wait_ge(lo_ready[slot(u)], c * 2)
                for dst, src in halves:
                    sp.dma_start(dst, src).then_inc(raw_landed[slot(u)], 16)

            def load_gate_up(name, i):
                for j in range(2):
                    u = UNIT[name] + j
                    load(u, cycle(u) + i,
                         [(w_raw[slot(u)][:, :, g * FB:(g + 1) * FB],
                           w_gu[name][:, 4 * j:4 * j + 4, g, bass.ds(i * FB, FB)]) for g in range(2)])

            def load_down(name, i):
                u = UNIT[name] + 2
                load(u, cycle(u) + i,
                     [(half(w_raw[slot(u)], b).rearrange("p n d -> p (n d)"),
                       w_dn[name][:, bass.ds(i * 2 + b, 1), :].rearrange("p c d -> p (c d)")) for b in range(2)])

            def load_dense(name, m):
                w = dense[name].rearrange("(k p) n -> p k n", p=P)
                n, j = m // 2, m % 2
                u = UNIT[name] + m
                load(u, cycle(u), [(half(w_raw[slot(u)], b),
                                    w[:, 4 * j + 2 * b:4 * j + 2 * b + 2, n * 512:(n + 1) * 512]) for b in range(2)])

            def first_two(name):
                if name.startswith("ffn"):
                    load_gate_up(name, 0)
                else:
                    load_dense(name, 0)
                    load_dense(name, 1)

            x_dram = a["x"][0].rearrange("(t p) d -> p t d", p=P)
            sp.dma_start(h[:, 0, :], x_dram[:, 0, :]).then_inc(x_landed, 16)
            first_two(STAGES[0])
            for name, following in zip(STAGES, STAGES[1:] + [None]):
                if name.startswith("ffn"):
                    load_gate_up(name, 1)
                    load_down(name, 0)
                    with sp.Fori(2, STEPS) as i:
                        load_gate_up(name, i)
                        load_down(name, i - 1)
                    if following is not None:
                        first_two(following)
                    load_down(name, STEPS - 1)
                else:
                    for m in range(2, dense[name].shape[1] // 256):
                        load_dense(name, m)
                    first_two(following)
            out_dram = out[0].rearrange("(t p) d -> p t d", p=P)
            for t in range(NT):
                sp.wait_ge(h_ready, 5 * NT + t + 1)
                sp.dma_start(out_dram[:, t, :], h[:, t, :]).then_inc(out_landed, 16)
            sp.wait_ge(out_landed, 16 * NT)

        gains = [a["ffn1_norm"][0], a["mem_norm"][0], a["mix_norm"][0], a["ffn2_norm"][0], a["kv_norm"],
                 a["ffn1_norm"][1], a["mem_norm"][1], a["mix_norm"][1], a["ffn2_norm"][1]]

        @block.gpsimd
        def _(pool):
            step = [0]

            def link(ins):
                step[0] += 1
                ins.then_inc(pool_step, 1)
                pool.wait_ge(pool_step, step[0])

            def load_gain(k):
                if k >= 2:
                    pool.wait_ge(xn_ready, (k - 2) * NT + NT)
                pool.dma_start(gain[:, k % 2, :], gains[k].partition_broadcast(P)).then_inc(gain_landed[k % 2], 16)

            def load_mem():
                pool.dma_start(ycat[:, :, :], a["mem"][0].rearrange("(t p) d -> p t d", p=P)).then_inc(mem_again_landed, 16)

            def row_roots(k):
                for t in range(NT):
                    c = (k % 2) * NT + t
                    pool.wait_ge(row_summed, k * NT + t + 1)
                    link(nc.gpsimd.tensor_scalar(row_ms[:, c:c + 1], row_ss[:, c:c + 1], 1.0 / D, EPS, ALU.mult, ALU.add))
                    nc.gpsimd.tensor_tensor(row_rs[:, c:c + 1], row_ms[:, c:c + 1], minus_half[:, 0:1],
                                            ALU.pow).then_inc(row_scaled, 1)

            def head_roots(name):
                x = HEADNORMS.index(name)
                n = head_view(name).shape[1] * head_view(name).shape[2]
                pool.wait_ge(head_summed, x + 1)
                link(nc.gpsimd.tensor_scalar(head_ms[:, 0:n], head_ss[:, 0:n], 1.0 / HD, EPS, ALU.mult, ALU.add))
                nc.gpsimd.tensor_tensor(head_rs[:, 0:n], head_ms[:, 0:n], minus_half[:, 0:n],
                                        ALU.pow).then_inc(head_scaled, 1)

            load_gain(0)
            pool.dma_start(ident[:, :], a["c_ident"]).then_inc(ident_landed, 16)
            link(nc.gpsimd.memset(minus_half[:, :], -0.5))
            nc.gpsimd.memset(head_gain_col[0:ROT, 2:3], 1.0).then_inc(ones_ready, 1)
            nc.gpsimd.memset(head_gain_col[0:ROT, 4:5], 1.0).then_inc(ones_ready, 1)
            row_roots(0)
            load_gain(1)
            small = [
                (inv_freq[:, :], a["c_inv_freq"].partition_broadcast(P)),
                (pos_i[:, 0:1], a["positions"][0, 0:P].rearrange("(p o) -> p o", o=1)),
                (pos_i[:, 1:2], a["positions"][0, P:S].rearrange("(p o) -> p o", o=1)),
                (band0, a["c_band0"]),
                (band1, a["c_band1"]),
                (inv_count[:, :, :], a["c_inv_count"]),
                (mask[:, :], a["c_mask"]),
                (pool_w, a["pool_w"][0].rearrange("g (c p) d -> p g c d", p=GC)),
                (pool_scale, a["pool_scale"][0].partition_broadcast(P)),
                (head_gain_col[:, 0:1], a["mem_k_norm"][0].rearrange("(p o) -> p o", o=1)),
                (head_gain_col[:, 1:2], a["mem_q_norm"][0].rearrange("(p o) -> p o", o=1)),
                (head_gain_col[ROT:HD, 2:3], a["k_norm"][ROT:HD].rearrange("(p o) -> p o", o=1)),
                (head_gain_col[:, 3:4], a["mem_k_norm"][1].rearrange("(p o) -> p o", o=1)),
                (head_gain_col[ROT:HD, 4:5], a["attn_q_norm"][0, ROT:HD].rearrange("(p o) -> p o", o=1)),
                (head_gain_col[:, 5:6], a["mem_q_norm"][1].rearrange("(p o) -> p o", o=1)),
                (rot_gain[:, 0, :], a["k_norm"][0:ROT].partition_broadcast(P)),
                (rot_gain[:, 1, :], a["attn_q_norm"][0, 0:ROT].partition_broadcast(P)),
                (sinks[:, :], a["attn_sinks"][0].partition_broadcast(P)),
            ]
            assert len(small) == SMALL_LOADS
            for dst, src in small:
                pool.dma_start(dst, src).then_inc(consts_landed, 16)
            row_roots(1)
            load_gain(2)
            row_roots(2)
            load_gain(3)
            head_roots("mk0")
            head_roots("mq0")
            pool.wait_ge(turned, split_index("Y0", 1, 1) + 1)
            load_mem()
            for k in (3, 4, 5, 6):
                row_roots(k)
                load_gain(k + 1)
            head_roots("k1")
            row_roots(7)
            load_gain(8)
            head_roots("mk1")
            head_roots("qa1")
            head_roots("qm1")
            row_roots(8)

        @block.scalar
        def _(act):
            def high(u, c, part=None):
                s = slot(u)
                act.wait_ge(raw_landed[s], (c + 1) * 32)
                for b in range(2) if part is None else (part,):
                    if not isinstance(c, int) or c > 0:
                        act.wait_ge(weights_used[s], c * 2 + (b - 1))
                    nc.scalar.copy(half(w_hi[s], b), half(w_raw[s], b)).then_inc(hi_ready[s], 1)

            def high_u(u):
                if u < UNITS:
                    high(u, cycle(u))

            def row_sum(k, t):
                src = h if NORMS[k][0] == "h" else ycat
                c = (k % 2) * NT + t
                if k == 0:
                    act.wait_ge(x_landed if t == 0 else x1_landed, 16)
                elif NORMS[k][0] == "mem":
                    act.wait_ge(mem_landed if k == 1 else mem_again_landed, 16)
                else:
                    act.wait_ge(h_ready, (RESID_BEFORE[k] - 1) * NT + t + 1)
                if k >= 2:
                    act.wait_ge(row_scaled, (k - 2) * NT + t + 1)
                if 2 * k + t > 0:
                    act.wait_ge(row_summed, 2 * k + t)
                nc.scalar.activation(squares[:, :], src[:, t, :], ACT.Square,
                                     accum_out=row_ss[:, c:c + 1]).then_inc(row_summed, 1)

            def split(name, t, dest):
                for b in range(2):
                    q = split_index(name, t, b)
                    act.wait_ge(turned, q + 1)
                    nc.scalar.copy(tr_hi[dest][:, 4 * b:4 * b + 4, t * P:(t + 1) * P],
                                   ps[:, TR_BANK + b, :].rearrange("p (k t) -> p k t", k=4)).then_inc(split_hi, 1)

            def silu(c, t, u, used):
                if t == 0:
                    act.wait_ge(gu_done, c + 1)
                else:
                    act.wait_ge(weights_used[slot(u + 1)], used * 2 + 2)
                nc.scalar.activation(silu_g[:, t, :], ps[:, GU_BANK + t, 0:FB], ACT.Silu).then_inc(silu_ready, 1)

            def actT_high(e):
                act.wait_ge(act_turned, e + 1)
                nc.scalar.copy(actT_hi[:, :, :, :].rearrange("p c t n -> p (c t n)"),
                               ps[:, TR_BANK, :]).then_inc(actT_hi_ready, 1)

            def ffn(f):
                u = UNIT[f"ffn{f}"]
                c0 = f * STEPS
                e0 = f * (STEPS + 1)

                def step(c, first=False):
                    if not first:
                        high(u + 2, c - 1 + cycle(u + 2))
                    silu(c0 + c, 0, u, None)
                    if not first:
                        actT_high(e0 + c - 1)
                    high(u, c + 1 + cycle(u))
                    silu(c0 + c, 1, u, cycle(u + 1) + c)
                    high(u + 1, c + 1 + cycle(u + 1))

                step(0, first=True)
                step(1)
                with act.Fori(2, STEPS - 1) as i:
                    step(i)
                last = STEPS - 1
                high(u + 2, last - 1 + cycle(u + 2))
                silu(c0 + last, 0, u, None)
                actT_high(e0 + last - 1)
                high_u(u + FFN_UNITS)
                silu(c0 + last, 1, u, cycle(u + 1) + last)
                high_u(u + FFN_UNITS + 1)
                for fc in range(2):
                    act.wait_ge(act_turned, e0 + last + fc + 1)
                    act.wait_ge(weights_used[slot(u + 2)], (last - 1 + cycle(u + 2)) * 2 + fc + 1)
                    nc.scalar.copy(actT_hi[:, fc, :, :].rearrange("p t n -> p (t n)"),
                                   ps[:, TR_BANK + fc, fc * FB:(fc + 1) * FB]).then_inc(actT_hi_ready, 1)
                    high(u + 2, last + cycle(u + 2), fc)

            def head_copy(y):
                name, part, bank, g = HEADTS[y]
                dst = {"mk0": mkT, "mk1": mkT, "k1": kT, "mq0": mqT, ("qm1", 1): mqT}.get(name if part == 0 else (name, part))
                first = 4 * part + (8 if name == "qm1" else 0)
                dst = qT[:, first:first + 4, :] if dst is None else dst[:, :, :]
                if y == 0:
                    act.wait_ge(consts_landed, 16 * SMALL_LOADS)
                    act.wait_ge(ones_ready, 2)
                act.wait_ge(head_turned, y + 1)
                nc.scalar.activation(dst.rearrange("p n t -> p (n t)"),
                                     ps[0:HD, bank:bank + 2, :].rearrange("p b n -> p (b n)"), ACT.Copy,
                                     scale=head_gain_col[:, g:g + 1]).then_inc(headT_ready, 1)

            def z_copy(l, n, t):
                product_done(act, t, z_done, l * 2 + n + 1, UNIT[f"z{l}"] + 2 * n + 1)
                nc.scalar.copy(xn[:, t, n * 512:(n + 1) * 512], ps[:, SUM_BANK + 2 * t + n, :]).then_inc(z_ready, 1)

            def exponentials(r):
                kind, t, h0, nh, width = ROUNDS[r]
                act.wait_ge(max_ready, r + 1)
                if r >= 2:
                    act.wait_ge(probs_turned, r - 1)
                    act.wait_ge(o_ready, r - 1)
                if kind == "band":
                    nc.scalar.activation(sink_p[:, r % 2, 0:nh], sink_p[:, r % 2, 0:nh], ACT.Exp)
                for n in range(nh):
                    ins = nc.scalar.activation(probs_view(r)[:, n, :], score_view(r)[:, n, :], ACT.Exp,
                                               bias=neg_max[:, r % 2, n:n + 1], scale=SM_SCALE,
                                               accum_out=den[:, r % 2, n:n + 1])
                ins.then_inc(probs_ready, 1)

            def attention(l):
                r0, r1 = LAYER_ROUNDS[l]
                for r in range(r0, r1):
                    exponentials(r)

            def proj_high(name, m):
                for j in range(m):
                    high_u(UNIT[name] + 2 + j)

            x_dram = a["x"][0].rearrange("(t p) d -> p t d", p=P)
            act.dma_start(h[:, 1, :], x_dram[:, 1, :]).then_inc(x1_landed, 16)
            act.dma_start(ycat[:, :, :], a["mem"][0].rearrange("(t p) d -> p t d", p=P)).then_inc(mem_landed, 16)
            row_sum(0, 0)
            row_sum(0, 1)
            high_u(0)
            split("N0", 0, "main")
            split("N0", 1, "main")
            high_u(1)
            row_sum(1, 0)
            row_sum(1, 1)
            split("N1", 0, "side")
            split("N1", 1, "side")
            act.wait_ge(angle_ready, 1)
            nc.scalar.activation(rope[:, 6, :, :], rope[:, 4, :, :], ACT.Sin)
            nc.scalar.activation(rope[:, 7, :, :], rope[:, 5, :, :], ACT.Sin).then_inc(rope_ready, 1)
            ffn(0)
            row_sum(2, 0)
            row_sum(2, 1)
            proj_high("mkv0", 2)
            split("N2", 0, "main")
            split("N2", 1, "main")
            high_u(UNIT["z0"] + 2)
            z_copy(0, 0, 0)
            high_u(UNIT["z0"] + 3)
            z_copy(0, 0, 1)
            high_u(UNIT["z0"] + 4)
            head_copy(0)
            z_copy(0, 1, 0)
            high_u(UNIT["z0"] + 5)
            z_copy(0, 1, 1)
            for c in range(4):
                act.wait_ge(pooled_done, c + 1)
                nc.scalar.copy(pooledT[:, 2 * c:2 * c + 2, :].rearrange("p c t -> p (c t)"),
                               ps[0:GC, GU_BANK + c, :]).then_inc(pooled_ready, 1)
            head_copy(1)
            act.wait_ge(pool_y_done, NT)
            attention(0)
            split("Y0", 0, "main")
            split("Y0", 1, "main")
            proj_high("out0", 4)
            row_sum(3, 0)
            row_sum(3, 1)
            split("N3", 0, "main")
            split("N3", 1, "main")
            ffn(1)
            row_sum(4, 0)
            row_sum(4, 1)
            row_sum(5, 0)
            row_sum(5, 1)
            row_sum(6, 0)
            row_sum(6, 1)
            split("N4", 0, "side")
            split("N4", 1, "side")
            split("N5", 0, "main")
            split("N5", 1, "main")
            proj_high("kv", 2)
            product_done(act, 1, None, None, UNIT["kv"] + 1)
            split("N6", 0, "side")
            split("N6", 1, "side")
            ffn(2)
            row_sum(7, 0)
            row_sum(7, 1)
            proj_high("mkv1", 2)
            split("N7", 0, "main")
            split("N7", 1, "main")
            high_u(UNIT["z1"] + 2)
            head_copy(2)
            z_copy(1, 0, 0)
            high_u(UNIT["z1"] + 3)
            z_copy(1, 0, 1)
            high_u(UNIT["z1"] + 4)
            head_copy(3)
            z_copy(1, 1, 0)
            high_u(UNIT["z1"] + 5)
            z_copy(1, 1, 1)
            for y in range(4, len(HEADTS)):
                head_copy(y)
            attention(1)
            split("Y1", 0, "main")
            split("Y1", 1, "main")
            proj_high("out1", 4)
            row_sum(8, 0)
            row_sum(8, 1)
            split("N8", 0, "main")
            split("N8", 1, "main")
            ffn(3)

        @block.vector
        def _(dve):
            step_count = [0]

            def link(ins):
                step_count[0] += 1
                ins.then_inc(dve_step, 1)
                dve.wait_ge(dve_step, step_count[0])

            def low(u, c, part=None):
                s = slot(u)
                for b in range(2) if part is None else (part,):
                    dve.wait_ge(hi_ready[s], c * 2 + (b + 1))
                    nc.vector.tensor_tensor(half(w_lo[s], b), half(w_raw[s], b), half(w_hi[s], b).bitcast(F32),
                                            ALU.subtract).then_inc(lo_ready[s], 1)

            def low_u(u):
                if u < UNITS:
                    low(u, cycle(u))

            def norm_rows(k, t):
                src = h if NORMS[k][0] == "h" else ycat
                c = (k % 2) * NT + t
                name = f"N{k}"
                if t == 0:
                    dve.wait_ge(gain_landed[k % 2], 16 * (k // 2 + 1))
                dve.wait_ge(row_scaled, k * NT + t + 1)
                q = split_index(name, t, 0)
                if q >= 2 * NT:
                    dve.wait_ge(turned, q - 2 * NT + 2)
                nc.vector.scalar_tensor_tensor(out=xn[:, t, :], in0=src[:, t, :], scalar=row_rs[:, c:c + 1],
                                               in1=gain[:, k % 2, :], op0=ALU.mult, op1=ALU.mult).then_inc(xn_ready, 1)

            def split(name, t, dest):
                for b in range(2):
                    q = split_index(name, t, b)
                    hi = tr_hi[dest][:, 4 * b:4 * b + 4, t * P:(t + 1) * P]
                    lo = tr_lo[dest][:, 4 * b:4 * b + 4, t * P:(t + 1) * P]
                    dve.wait_ge(split_hi, q + 1)
                    nc.vector.tensor_tensor(lo, ps[:, TR_BANK + b, :].rearrange("p (k t) -> p k t", k=4),
                                            hi.bitcast(F32), ALU.subtract).then_inc(split_lo, 1)

            def gated(c, t, turned_before):
                dve.wait_ge(silu_ready, c * 2 + (t + 1))
                if turned_before is not None:
                    dve.wait_ge(act_turned, turned_before)
                nc.vector.tensor_tensor(act_f[:, t, :], ps[:, GU_BANK + t, FB:2 * FB], silu_g[:, t, :],
                                        ALU.mult).then_inc(act_ready, 1)

            def actT_low(e):
                dve.wait_ge(actT_hi_ready, e + 1)
                nc.vector.tensor_tensor(actT_lo[:, :, :, :].rearrange("p c t n -> p (c t n)"), ps[:, TR_BANK, :],
                                        actT_hi[:, :, :, :].rearrange("p c t n -> p (c t n)").bitcast(F32),
                                        ALU.subtract).then_inc(actT_lo_ready, 1)

            def ffn(f):
                u = UNIT[f"ffn{f}"]
                c0 = f * STEPS

                e0 = f * (STEPS + 1)

                def step(c, first=False):
                    if not first:
                        low(u + 2, c - 1 + cycle(u + 2))
                    gated(c0 + c, 0, None if first else e0 + c)
                    if not first:
                        actT_low(e0 + c - 1)
                    low(u, c + 1 + cycle(u))
                    gated(c0 + c, 1, None)
                    low(u + 1, c + 1 + cycle(u + 1))

                step(0, first=True)
                step(1)
                with dve.Fori(2, STEPS - 1) as i:
                    step(i)
                last = STEPS - 1
                low(u + 2, last - 1 + cycle(u + 2))
                gated(c0 + last, 0, e0 + last)
                actT_low(e0 + last - 1)
                low_u(u + FFN_UNITS)
                gated(c0 + last, 1, None)
                low_u(u + FFN_UNITS + 1)
                for fc in range(2):
                    dve.wait_ge(actT_hi_ready, e0 + last + fc + 1)
                    nc.vector.tensor_tensor(actT_lo[:, fc, :, :].rearrange("p t n -> p (t n)"),
                                            ps[:, TR_BANK + fc, fc * FB:(fc + 1) * FB],
                                            actT_hi[:, fc, :, :].rearrange("p t n -> p (t n)").bitcast(F32),
                                            ALU.subtract).then_inc(actT_lo_ready, 1)
                    low(u + 2, last + cycle(u + 2), fc)

            def residual(r, weight):
                for t in range(NT):
                    product_done(dve, t, sum_done, r + 1, sum_units[r])
                    nc.vector.scalar_tensor_tensor(
                        out=h[:, t, :], in0=ps[:, SUM_BANK + 2 * t:SUM_BANK + 2 * t + 2, :].rearrange("p b n -> p (b n)"),
                        scalar=weight, in1=h[:, t, :], op0=ALU.mult, op1=ALU.add).then_inc(h_ready, 1)

            def proj_low(name, m):
                for j in range(m):
                    low_u(UNIT[name] + 2 + j)

            def kv_copy(dst, done, ready, base, name):
                for t in range(NT):
                    product_done(dve, t, done, base // NT + 1, UNIT[name] + 1)
                    nc.vector.tensor_copy(dst[:, t, :], ps[:, GU_BANK + t, :]).then_inc(ready, 1)
                dve.wait_ge(ready, base + NT)

            def head_norm(name):
                x = HEADNORMS.index(name)
                v = head_view(name)
                nt, nh = v.shape[1], v.shape[2]
                n = nt * nh
                sq = pT[:, 0:n * HD].rearrange("p (n d) -> p n d", d=HD)
                rs = head_rs[:, 0:n].rearrange("p (t n) -> p t n", t=nt).unsqueeze(3).to_broadcast([P, nt, nh, HD])
                link(nc.vector.tensor_tensor(sq.rearrange("p (t n) d -> p t n d", t=nt), v, v, ALU.mult))
                nc.vector.tensor_reduce(head_ss[:, 0:n], sq, AX.X, ALU.add).then_inc(head_summed, 1)
                dve.wait_ge(head_scaled, x + 1)
                ins = nc.vector.tensor_tensor(v, v, rs, ALU.mult)
                if name[:-1] in ("mk", "mq"):
                    ins.then_inc(head_ready, 1)
                    return
                link(ins)
                nh = min(nh, 4) if name == "qm1" else nh
                n = nt * nh
                v = v[:, :, 0:nh, :]
                g = rot_gain[:, 0 if name == "k1" else 1, :].unsqueeze(1).unsqueeze(1).to_broadcast([P, nt, nh, ROT])
                link(nc.vector.tensor_tensor(v[:, :, :, 0:ROT], v[:, :, :, 0:ROT], g, ALU.mult))
                x1, x2 = v[:, :, :, 0:RH], v[:, :, :, RH:ROT]
                cos, sin = (rope[:, i, :, :].unsqueeze(2).to_broadcast([P, nt, nh, RH]) for i in (6, 7))
                tmp = [rot[:, i, 0:n * RH].rearrange("p (t n d) -> p t n d", t=nt, n=nh) for i in range(4)]
                nc.vector.tensor_tensor(tmp[0], x1, cos, ALU.mult)
                nc.vector.tensor_tensor(tmp[1], x2, sin, ALU.mult)
                nc.vector.tensor_tensor(tmp[2], x2, cos, ALU.mult)
                link(nc.vector.tensor_tensor(tmp[3], x1, sin, ALU.mult))
                link(nc.vector.tensor_tensor(x1, tmp[0], tmp[1], ALU.subtract))
                nc.vector.tensor_tensor(x2, tmp[2], tmp[3], ALU.add).then_inc(head_ready, 1)

            def rope_tables():
                dve.wait_ge(consts_landed, 16 * SMALL_LOADS)
                pos, ang, whole, part, to_cos, to_sin = (rope[:, i, :, :] for i in range(6))
                posf = pos.rearrange("p t d -> p (t d)")[:, 0:NT]
                q1, q2, q3 = two_pi_parts()
                link(nc.vector.tensor_copy(posf, pos_i[:, :]))
                link(nc.vector.tensor_tensor(ang, posf.unsqueeze(2).to_broadcast([P, NT, RH]),
                                             inv_freq[:, :].unsqueeze(1).to_broadcast([P, NT, RH]), ALU.mult))
                link(nc.vector.tensor_scalar(whole, ang, 1.0 / (4096 * 2 * np.pi), MAGIC, ALU.mult, ALU.add))
                link(nc.vector.tensor_scalar(whole, whole, -MAGIC, 4096.0, ALU.add, ALU.mult))

                def less(turns, q):
                    link(nc.vector.scalar_tensor_tensor(out=ang, in0=turns, scalar=-q, in1=ang, op0=ALU.mult, op1=ALU.add))

                less(whole, q1)
                less(whole, q2)
                link(nc.vector.tensor_scalar(part, ang, 1.0 / (2 * np.pi), MAGIC, ALU.mult, ALU.add))
                link(nc.vector.tensor_scalar(part, part, -MAGIC, None, ALU.add))
                less(part, q1)
                less(part, q2)
                less(whole, q3)
                less(part, q3)
                link(nc.vector.tensor_scalar(to_sin, ang, 3.1415925, -3.1415925, ALU.min, ALU.max))
                link(nc.vector.tensor_scalar(part, to_sin, -1.0, None, ALU.mult))
                link(nc.vector.tensor_tensor(to_cos, part, to_sin, ALU.min))
                nc.vector.tensor_scalar(to_cos, to_cos, float(np.pi / 2), None, ALU.add).then_inc(angle_ready, 1)

            def maxima(r):
                kind, t, h0, nh, width = ROUNDS[r]
                mx, neg = row_max[:, r % 2, 0:nh], neg_max[:, r % 2, 0:nh]
                dve.wait_ge(score_done, r + 1)
                if r >= 2:
                    dve.wait_ge(probs_ready, r - 1)
                link(nc.vector.tensor_reduce(mx, score_view(r), AX.X, ALU.max))
                if kind == "band":
                    s = sinks[:, h0:h0 + nh]
                    link(nc.vector.scalar_tensor_tensor(out=mx, in0=mx, scalar=SM_SCALE, in1=s, op0=ALU.mult, op1=ALU.max))
                    link(nc.vector.tensor_tensor(sink_p[:, r % 2, 0:nh], s, mx, ALU.subtract))
                    nc.vector.tensor_scalar(neg, mx, -1.0, None, ALU.mult).then_inc(max_ready, 1)
                else:
                    nc.vector.tensor_scalar(neg, mx, -SM_SCALE, None, ALU.mult).then_inc(max_ready, 1)

            def probs_copy(r):
                kind, t, h0, nh, width = ROUNDS[r]
                dn = den[:, r % 2, 0:nh]
                dve.wait_ge(probs_turned, r + 1)
                if r > 0:
                    dve.wait_ge(o_done, r)
                nc.vector.tensor_copy(pT[:, 0:nh * width], ps[:, PT_BANK:PT_BANK + 2, :].rearrange("p b n -> p (b n)")[:, 0:nh * width]
                                      ).then_inc(pT_ready, 1)
                dve.wait_ge(probs_ready, r + 1)
                if kind == "band":
                    link(nc.vector.tensor_tensor(dn, dn, sink_p[:, r % 2, 0:nh], ALU.add))
                link(nc.vector.reciprocal(dn, dn))

            def output(r):
                kind, t, h0, nh, width = ROUNDS[r]
                base = h0 * HD + (MIXER if kind == "mem" else 0)
                dve.wait_ge(o_done, r + 1)
                nc.vector.tensor_tensor(
                    ycat[:, t, base:base + nh * HD].rearrange("p (n d) -> p n d", d=HD),
                    ps[:, O_BANK + r % 2, 0:nh * HD].rearrange("p (n d) -> p n d", d=HD),
                    den[:, r % 2, 0:nh].unsqueeze(2).to_broadcast([P, nh, HD]), ALU.mult).then_inc(o_ready, 1)

            def attention(l):
                r0, r1 = LAYER_ROUNDS[l]
                maxima(r0)
                maxima(r0 + 1)
                for r in range(r0, r1):
                    probs_copy(r)
                    if r + 2 < r1:
                        maxima(r + 2)
                    output(r)

            norm_rows(0, 0)
            norm_rows(0, 1)
            low_u(0)
            split("N0", 0, "main")
            split("N0", 1, "main")
            low_u(1)
            norm_rows(1, 0)
            norm_rows(1, 1)
            split("N1", 0, "side")
            split("N1", 1, "side")
            rope_tables()
            ffn(0)
            residual(0, 0.5)
            norm_rows(2, 0)
            norm_rows(2, 1)
            proj_low("mkv0", 2)
            kv_copy(mkv_sb, mkv_done, mkv_ready, 0, "mkv0")
            split("N2", 0, "main")
            split("N2", 1, "main")
            head_norm("mk0")
            proj_low("z0", 4)
            dve.wait_ge(z_ready, 2 * NT)
            head_norm("mq0")
            for t in range(NT):
                for g in range(GROUPS):
                    dve.wait_ge(pool_y_done, t + 1)
                    nc.vector.scalar_tensor_tensor(
                        out=ycat[:, t, g * GW:(g + 1) * GW],
                        in0=ps[:, GU_BANK + 2 * t + g // 2, (g % 2) * GW:(g % 2 + 1) * GW],
                        scalar=inv_count[:, t, g:g + 1], in1=pool_scale[:, g * GW:(g + 1) * GW],
                        op0=ALU.mult, op1=ALU.mult).then_inc(pool_y_ready, 1)
            attention(0)
            split("Y0", 0, "main")
            split("Y0", 1, "main")
            proj_low("out0", 4)
            residual(1, 1.0)
            norm_rows(3, 0)
            norm_rows(3, 1)
            split("N3", 0, "main")
            split("N3", 1, "main")
            ffn(1)
            residual(2, 0.5)
            norm_rows(4, 0)
            norm_rows(4, 1)
            split("N4", 0, "side")
            norm_rows(5, 0)
            split("N4", 1, "side")
            norm_rows(5, 1)
            split("N5", 0, "main")
            norm_rows(6, 0)
            split("N5", 1, "main")
            norm_rows(6, 1)
            proj_low("kv", 2)
            kv_copy(kv_sb, kv_done, kv_ready, 0, "kv")
            nc.vector.tensor_copy(v_mixed[0:CHUNK, :], kv_sb[0:CHUNK, 1, 256:512]).then_inc(mixed_ready, 1)
            nc.vector.tensor_copy(v_mixed[CHUNK:P, :], kv_sb[CHUNK:P, 0, 256:512]).then_inc(mixed_ready, 1)
            split("N6", 0, "side")
            split("N6", 1, "side")
            ffn(2)
            residual(3, 0.5)
            dve.wait_ge(rope_ready, 1)
            head_norm("k1")
            norm_rows(7, 0)
            norm_rows(7, 1)
            proj_low("mkv1", 2)
            kv_copy(mkv_sb, mkv_done, mkv_ready, NT, "mkv1")
            split("N7", 0, "main")
            split("N7", 1, "main")
            low_u(UNIT["z1"] + 2)
            head_norm("mk1")
            low_u(UNIT["z1"] + 3)
            low_u(UNIT["z1"] + 4)
            dve.wait_ge(z_ready, 3 * NT)
            head_norm("qa1")
            low_u(UNIT["z1"] + 5)
            dve.wait_ge(z_ready, 4 * NT)
            head_norm("qm1")
            attention(1)
            split("Y1", 0, "main")
            split("Y1", 1, "main")
            proj_low("out1", 4)
            residual(4, 1.0)
            norm_rows(8, 0)
            norm_rows(8, 1)
            split("N8", 0, "main")
            split("N8", 1, "main")
            ffn(3)
            residual(5, 0.5)

        @block.tensor
        def _(pe):
            def turn(name, src, ready, value):
                for t in range(NT):
                    pe.wait_ge(ready, value(t))
                    for b in range(2):
                        q = split_index(name, t, b)
                        if q >= 2:
                            pe.wait_ge(split_lo, q - 1)
                        for k in range(4):
                            c = (4 * b + k) * P
                            mm = pe.transpose(ps[:, TR_BANK + b, k * P:(k + 1) * P], src[:, t, c:c + P], ident[:, :])
                        mm.then_inc(turned, 1)

            def turn_norm(k):
                turn(f"N{k}", xn, xn_ready, lambda t: k * NT + t + 1)

            def three(dst, x_hi, x_lo, wh, wl, start, stop):
                pe.matmul(dst, x_hi, wh, start=start, stop=False)
                pe.matmul(dst, x_hi, wl, start=False, stop=False)
                return pe.matmul(dst, x_lo, wh, start=False, stop=stop)

            def product(u, c, t, dst, src, split_name, wait_src):
                for k in range(KC):
                    s = slot(u + k // 4)
                    kk = k % 4
                    if wait_src and k % 4 == 0:
                        pe.wait_ge(split_lo, split_index(split_name, t, k // 4) + 1)
                    if t == 0 and kk % 2 == 0:
                        pe.wait_ge(lo_ready[s], c[k // 4] * 2 + (kk // 2 + 1))
                    mm = three(dst, tr_hi[src][:, k, t * P:(t + 1) * P], tr_lo[src][:, k, t * P:(t + 1) * P],
                               w_hi[s][:, kk, :], w_lo[s][:, kk, :], k == 0, k == KC - 1)
                    if t == NT - 1 and kk % 2 == 1:
                        if k == KC - 1:
                            return mm, s
                        mm.then_inc(weights_used[s], 1)
                return mm, None

            def projection(name, src, split_name, bank, done, order, blocks=None, tiles=(0, 1)):
                if blocks is None:
                    blocks = range(2) if name in ("z0", "z1", "out0", "out1") else range(1)
                for n in blocks:
                    for t in tiles:
                        u = UNIT[name] + 2 * n
                        mm, s = product(u, (cycle(u), cycle(u + 1)), t, ps[:, bank(t, n), :], src, split_name, n == 0)
                        if s is not None:
                            mm.then_inc(weights_used[s], 1)
                        elif order(n):
                            mm.then_inc(done, 1)

            def ffn(f, split_name):
                u = UNIT[f"ffn{f}"]
                c0 = f * STEPS
                e0 = f * (STEPS + 1)

                def gate_up(c, t, first=False):
                    if not first or f > 0:
                        pe.wait_ge(act_ready, (c0 + c) * 2 + (t - 1))
                    mm, s = product(u, (cycle(u) + c, cycle(u + 1) + c), t, ps[:, GU_BANK + t, :], "main", split_name, first)
                    mm.then_inc(gu_done if s is None else weights_used[s], 1)

                def turn_act(c, split=False):
                    pe.wait_ge(act_ready, (c0 + c) * 2 + 2)
                    for fc in range(2):
                        bank = TR_BANK + (fc if split else 0)
                        for t in range(NT):
                            mm = pe.transpose(ps[:, bank, (fc * NT + t) * P:(fc * NT + t + 1) * P],
                                              act_f[:, t, fc * P:(fc + 1) * P], ident[:, :])
                        if split or fc == 1:
                            mm.then_inc(act_turned, 1)

                def down(c, fc, parts, first=False, last=False):
                    s = slot(u + 2)
                    if parts == 2 or fc == 0:
                        pe.wait_ge(actT_lo_ready, e0 + c + (1 + (fc if parts == 2 else 0)))
                    pe.wait_ge(lo_ready[s], (cycle(u + 2) + c) * 2 + (fc + 1))
                    for t in range(NT):
                        xh, xl = actT_hi[:, fc, t, :], actT_lo[:, fc, t, :]
                        wh = [w_hi[s][:, 2 * fc + n, :] for n in range(2)]
                        wl = [w_lo[s][:, 2 * fc + n, :] for n in range(2)]
                        dst = [ps[:, SUM_BANK + 2 * t + n, :] for n in range(2)]
                        for n in range(2):
                            pe.matmul(dst[n], xh, wh[n], start=first and fc == 0, stop=False)
                        for n in range(2):
                            pe.matmul(dst[n], xh, wl[n], start=False, stop=False)
                        for n in range(2):
                            mm = pe.matmul(dst[n], xl, wh[n], start=False, stop=last and fc == 1)
                        if t == NT - 1:
                            mm.then_inc(weights_used[s], 1)
                        elif last and fc == 1:
                            mm.then_inc(sum_done, 1)

                gate_up(0, 0, first=True)
                gate_up(0, 1, first=True)
                gate_up(1, 0)
                turn_act(0)
                gate_up(1, 1)
                down(0, 0, 1, first=True)
                down(0, 1, 1)
                last = STEPS - 1
                with pe.Fori(2, last) as i:
                    gate_up(i, 0)
                    turn_act(i - 1)
                    gate_up(i, 1)
                    down(i - 1, 0, 1)
                    down(i - 1, 1, 1)
                gate_up(last, 0)
                turn_act(last - 1)
                gate_up(last, 1)
                down(last - 1, 0, 1)
                turn_act(last, split=True)
                down(last - 1, 1, 1)
                down(last, 0, 2)
                down(last, 1, 2, last=True)

            def turn_heads(y):
                name, part, bank, _ = HEADTS[y]
                v = head_view(name)
                pe.wait_ge(head_ready, HEADNORMS.index(name) + 1)
                if y >= 2:
                    pe.wait_ge(headT_ready, y - 1)
                dst = ps[0:HD, bank:bank + 2, :].rearrange("p b (n t k) -> p (b n) t k", n=2, t=NT)
                for n in range(4):
                    for t in range(NT):
                        mm = pe.transpose(dst[:, n, t, :], v[:, t, 4 * part + n, :], ident[:, :])
                mm.then_inc(head_turned, 1)

            def scores(r):
                kind, t, h0, nh, width = ROUNDS[r]
                dst = score_view(r)
                if r - 2 >= 0:
                    pe.wait_ge(probs_ready, r - 1)
                if kind == "band" and t == 0:
                    for n in range(0, nh, 4):
                        pe.matmul(dst[:, n:n + 4, :], ident[:, :], mask[:, :].unsqueeze(1).to_broadcast([P, 4, P]),
                                  start=True, stop=False)
                for n in range(nh):
                    if kind == "mem":
                        mm = pe.matmul(dst[:, n, :], mqT[:, n, t * P:(t + 1) * P], mkT[:, n, :], start=True, stop=True)
                        continue
                    q, k = qT[:, h0 + n, :], kT[:, (h0 + n) // GQA, :]
                    if t == 0:
                        mm = pe.matmul(dst[:, n, :], q[:, 0:P], k[:, 0:P], start=False, stop=(n % 4 == 3))
                    else:
                        pe.matmul(dst[0:CHUNK, n, 0:CHUNK], q[:, P:P + CHUNK], k[:, P:P + CHUNK], start=True, stop=True)
                        pe.matmul(dst[0:CHUNK, n, CHUNK:P], q[:, P:P + CHUNK], k[:, CHUNK:P], start=True, stop=True)
                        mm = pe.matmul(dst[CHUNK:P, n, :], q[:, P + CHUNK:S], k[:, P:S], start=True, stop=True)
                mm.then_inc(score_done, 1)

            def turn_probs(r):
                kind, t, h0, nh, width = ROUNDS[r]
                flat = ps[:, PT_BANK:PT_BANK + 2, :].rearrange("p b n -> p (b n)")
                pe.wait_ge(probs_ready, r + 1)
                if r > 0:
                    pe.wait_ge(pT_ready, r)
                for j in range(nh * width // P):
                    mm = pe.transpose(flat[:, j * P:(j + 1) * P], probs[:, r % 2, j * P:(j + 1) * P], ident[:, :])
                mm.then_inc(probs_turned, 1)

            def values(r):
                kind, t, h0, nh, width = ROUNDS[r]
                pe.wait_ge(pT_ready, r + 1)
                if r >= 2:
                    pe.wait_ge(o_ready, r - 1)
                for n in range(nh):
                    dst = ps[:, O_BANK + r % 2, n * HD:(n + 1) * HD]
                    if kind == "mem":
                        v = mkv_sb[:, :, 256 + n * HD:256 + (n + 1) * HD]
                        for b in range(2):
                            j = (2 * n + b) * P
                            mm = pe.matmul(dst, pT[:, j:j + P], v[:, b, :], start=(b == 0), stop=(b == 1))
                        continue
                    g = (h0 + n) // GQA * HD
                    v = kv_sb[:, t, 256 + g:256 + g + HD]
                    if t == 0:
                        mm = pe.matmul(dst, pT[:, n * P:(n + 1) * P], v, start=True, stop=True)
                    else:
                        pe.matmul(dst[0:CHUNK, :], pT[:, n * P:n * P + CHUNK], v_mixed[:, g:g + HD], start=True, stop=True)
                        mm = pe.matmul(dst[CHUNK:P, :], pT[:, n * P + CHUNK:(n + 1) * P], v, start=True, stop=True)
                mm.then_inc(o_done, 1)

            def attention(l, scored=False):
                r0, r1 = LAYER_ROUNDS[l]
                if not scored:
                    scores(r0)
                    scores(r0 + 1)
                for r in range(r0, r1):
                    turn_probs(r)
                    if r + 2 < r1:
                        scores(r + 2)
                    values(r)

            def pooled(c0, c1):
                for c in range(c0, c1):
                    dst = ps[0:GC, GU_BANK + c // 2, (c % 2) * S:(c % 2 + 1) * S]
                    cols = slice(c * GC, (c + 1) * GC)
                    pe.matmul(dst, xn[:, 0, cols], band0[:, c // 2, :], start=True, stop=False)
                    mm = pe.matmul(dst[:, P:S], xn[:, 1, cols], band1[:, c // 2, :], start=False, stop=True)
                    if c % 2 == 1:
                        mm.then_inc(pooled_done, 1)

            def pool_products():
                pe.wait_ge(pooled_ready, 4)
                for t in range(NT):
                    for g in range(GROUPS):
                        dst = ps[:, GU_BANK + 2 * t + g // 2, (g % 2) * GW:(g % 2 + 1) * GW]
                        for c in range(2):
                            mm = pe.matmul(dst, pooledT[:, 2 * g + c, t * P:(t + 1) * P], pool_w[:, g, c, :],
                                           start=(c == 0), stop=(c == 1))
                    mm.then_inc(pool_y_done, 1)

            def to_gu(t, n):
                return GU_BANK + t

            def to_sum(t, n):
                return SUM_BANK + 2 * t + n

            pe.wait_ge(ident_landed, 16)
            turn_norm(0)
            turn_norm(1)
            ffn(0, "N0")
            projection("mkv0", "side", "N1", to_gu, mkv_done, lambda n: True)
            turn_norm(2)
            pe.wait_ge(h_ready, NT)
            z0 = ("z0", "main", "N2", to_sum, z_done, lambda n: True)
            projection(*z0, blocks=(0,))
            turn_heads(0)
            projection(*z0, blocks=(1,), tiles=(0,))
            pe.wait_ge(consts_landed, 16 * SMALL_LOADS)
            pe.wait_ge(z_ready, NT)
            pe.wait_ge(mkv_ready, NT)
            pooled(0, 4)
            projection(*z0, blocks=(1,), tiles=(1,))
            pe.wait_ge(headT_ready, 1)
            pe.wait_ge(z_ready, 2 * NT)
            pooled(4, 8)
            turn_heads(1)
            pool_products()
            pe.wait_ge(headT_ready, 2)
            r0 = LAYER_ROUNDS[0][0]
            scores(r0)
            scores(r0 + 1)
            pe.wait_ge(pool_y_ready, NT * GROUPS)
            attention(0, scored=True)
            turn("Y0", ycat, o_ready, lambda t: LAYER_ROUNDS[0][1])
            projection("out0", "main", "Y0", to_sum, sum_done, lambda n: n == 1)
            turn_norm(3)
            ffn(1, "N3")
            turn_norm(4)
            turn_norm(5)
            projection("kv", "side", "N4", to_gu, kv_done, lambda n: True)
            turn_norm(6)
            pe.wait_ge(kv_ready, NT)
            ffn(2, "N5")
            projection("mkv1", "side", "N6", to_gu, mkv_done, lambda n: True)
            turn_norm(7)
            pe.wait_ge(h_ready, 4 * NT)
            z1 = ("z1", "main", "N7", to_sum, z_done, lambda n: True)
            projection(*z1, blocks=(0,))
            turn_heads(2)
            pe.wait_ge(mkv_ready, 2 * NT)
            projection(*z1, blocks=(1,), tiles=(0,))
            turn_heads(3)
            projection(*z1, blocks=(1,), tiles=(1,))
            for y in range(4, len(HEADTS)):
                turn_heads(y)
            pe.wait_ge(headT_ready, len(HEADTS))
            pe.wait_ge(mixed_ready, 2)
            attention(1)
            turn("Y1", ycat, o_ready, lambda t: LAYER_ROUNDS[1][1])
            projection("out1", "main", "Y1", to_sum, sum_done, lambda n: n == 1)
            turn_norm(8)
            ffn(3, "N8")


_INS = ['x', 'mem', 'positions', 'ffn1_norm', 'ffn1_w_gate_up', 'ffn1_w_down', 'mix_norm', 'w_in', 'w_out',
        'pool_w', 'pool_scale', 'attn_q_norm', 'attn_sinks', 'kv_norm', 'w_kv', 'k_norm',
        'mem_norm', 'w_mem_kv', 'mem_q_norm', 'mem_k_norm', 'ffn2_norm', 'ffn2_w_gate_up', 'ffn2_w_down']


def kernel(**inputs):
    import numpy as _np
    import concourse.bacc as _bacc
    from concourse import mybir as _mybir
    from concourse.bass_utils import run_bass_kernel_spmd as _run

    nc = _bacc.Bacc("TRN2", target_bir_lowering=False, num_devices=1)
    arrays, aps = {}, {}
    for name, value in [(n, inputs[n]) for n in _INS] + list(shape_constants().items()):
        v = _np.ascontiguousarray(value)
        arrays[f"in_{name}_dram"] = v
        aps[name] = nc.dram_tensor(f"in_{name}_dram", v.shape, _mybir.dt.from_np(v.dtype), kind="ExternalInput").ap()
    out = nc.dram_tensor("out_0_dram", (1, S, D), _mybir.dt.float32, kind="ExternalOutput").ap()
    encoder_kernel(nc, aps, out)
    r = _run(nc, [arrays], core_ids=[0])
    return r.results[0]["out_0_dram"]
```

```python
from contextlib import ExitStack

import numpy as np

import concourse.bass as bass
from concourse import mybir

F32 = mybir.dt.float32
F32R = mybir.dt.float32r
I32 = mybir.dt.int32
ALU = mybir.AluOpType
ACT = mybir.ActivationFunctionType
AX = mybir.AxisListType

P = 128
D = 1024
S = 256
NT = S // P
KC = D // P
FF = ((8 * D // 3 + 127) // 128) * 128
FB = 256
STEPS = FF // FB
HD = 64
MIXER = 768
NHA = MIXER // HD
KVH = 4
GQA = NHA // KVH
MEMH = 4
GROUPS = 4
GW = MIXER // GROUPS
GC = GW // 2
WINDOWS = (2, 4, 8, 16)
CHUNK = 64
ROT = HD // 4
RH = ROT // 2
EPS = 1e-6
NEG_INF = -1e30
SM_SCALE = HD ** -0.5
SLOTS = 3
WARM_PRODUCTS = 13
MAGIC = 1.5 * 2.0 ** 23

SUM_BANK = 0
GU_BANK = 4
TR_BANK = 6
PT_BANK = 4
O_BANK = 6


def two_pi_parts():
    a = np.floor(2 * np.pi * 2 ** 9) / 2 ** 9
    b = np.floor((2 * np.pi - a) * 2 ** 22) / 2 ** 22
    return float(a), float(b), float(2 * np.pi - a - b)


FFN_UNITS = 3 * STEPS
UNIT = {}
_u = 0
for _name, _n in (("ffn0", FFN_UNITS), ("mkv0", 2), ("z0", 4), ("out0", 4), ("ffn1", FFN_UNITS), ("kv", 2),
                  ("ffn2", FFN_UNITS), ("mkv1", 2), ("z1", 4), ("out1", 4), ("ffn3", FFN_UNITS)):
    UNIT[_name] = _u
    _u += _n
UNITS = _u
STAGES = list(UNIT)

NORMS = [("h", "main"), ("mem", "side"), ("h", "main"), ("h", "main"), ("h", "side"), ("h", "main"),
         ("mem", "side"), ("h", "main"), ("h", "main")]
SPLITS = ["N0", "N1", "N2", "Y0", "N3", "N4", "N5", "N6", "N7", "Y1", "N8"]
RESID_BEFORE = {0: 0, 2: 1, 3: 2, 4: 3, 5: 3, 7: 4, 8: 5}

HEADNORMS = ["mk0", "mq0", "k1", "mk1", "qa1", "qm1"]
HEADREADY = ["mk0", "k1", "mk1", "qa1", "qm1"]
HEADTS = [("mk0", 0, 6, 0), ("mq0", 0, 0, 1), ("k1", 0, 6, 2), ("mk1", 0, 4, 3),
          ("qa1", 0, 6, 4), ("qa1", 1, 4, 4), ("qm1", 1, 4, 5), ("qm1", 0, 6, 4)]

ROUNDS = [("mem", 0, 0, MEMH, 2 * P), ("mem", 1, 0, MEMH, 2 * P),
          ("band", 0, 0, 8, P), ("band", 1, 0, 8, P), ("band", 0, 8, 4, P), ("band", 1, 8, 4, P),
          ("mem", 0, 0, MEMH, 2 * P), ("mem", 1, 0, MEMH, 2 * P)]
LAYER_ROUNDS = [(0, 2), (2, 8)]
SMALL_LOADS = 18
SOFT = 1024


def shape_constants():
    ident = np.eye(P, dtype=np.float32)
    t = np.arange(S)
    band = np.zeros((S, GROUPS, S), np.float32)
    inv_count = np.zeros((S, GROUPS), np.float32)
    for g, w in enumerate(WINDOWS):
        count = np.minimum(t + 1, w)
        inside = (t[:, None] <= t[None, :]) & (t[:, None] > t[None, :] - w)
        band[:, g, :] = inside.astype(np.float32)
        band[t, g, t] -= count.astype(np.float32)
        inv_count[:, g] = (1.0 / count).astype(np.float32)
    mask = np.where(t[:P, None] // CHUNK >= t[None, :P] // CHUNK, 0.0, NEG_INF).astype(np.float32)
    expo = -np.arange(0, ROT, 2, dtype=np.float32) / np.float32(ROT)
    inv_freq = (500000.0 ** expo.astype(np.float64)).astype(np.float32)
    return {
        "c_ident": ident,
        "c_band0": np.ascontiguousarray(band[0:P]),
        "c_band1": np.ascontiguousarray(band[P:S, :, P:S]),
        "c_inv_count": np.ascontiguousarray(inv_count.reshape(NT, P, GROUPS).transpose(1, 0, 2)),
        "c_mask": mask,
        "c_inv_freq": inv_freq,
    }


def encoder_kernel(nc, a, out):
    with ExitStack() as ctx:
        def sb(name, shape, dt=F32):
            return ctx.enter_context(nc.sbuf_tensor(name, shape, dt))

        def sem(name):
            return ctx.enter_context(nc.semaphore(name))

        ps = ctx.enter_context(nc.psum_tensor("ps", [P, 8, 512], F32))

        w_raw = [sb(f"w_raw{s}", [P, 4, 512]) for s in range(SLOTS)]
        w_hi = [sb(f"w_hi{s}", [P, 4, 512], F32R) for s in range(SLOTS)]
        w_lo = [sb(f"w_lo{s}", [P, 4, 512], F32R) for s in range(SLOTS)]
        h = sb("h", [P, NT, D])
        xn = sb("xn", [P, NT, D])
        ycat = sb("ycat", [P, NT, D])
        tr_hi = {n: sb(f"{n}T_hi", [P, KC, S], F32R) for n in ("main", "side")}
        tr_lo = {n: sb(f"{n}T_lo", [P, KC, S], F32R) for n in ("main", "side")}
        gain = sb("gain", [P, 2, D])
        silu_g = sb("silu_g", [P, NT, FB])
        act_f = sb("act_f", [P, NT, FB])
        actT_hi = sb("actT_hi", [P, 2, NT, P], F32R)
        actT_lo = sb("actT_lo", [P, 2, NT, P], F32R)
        kv_sb = sb("kv_sb", [P, NT, 512])
        mkv_sb = sb("mkv_sb", [P, NT, 512])
        kT = sb("kT", [HD, KVH, S])
        mkT = sb("mkT", [HD, MEMH, S])
        mqT = sb("mqT", [HD, MEMH, S])
        shared = sb("shared", [P, 3840])
        band0 = shared[:, 0:1024].rearrange("p (g t) -> p g t", g=GROUPS)
        band1 = shared[:, 1024:1536].rearrange("p (g t) -> p g t", g=GROUPS)
        pool_w = shared[0:GC, 1536:3072].rearrange("p (g c d) -> p g c d", g=GROUPS, c=2)
        pool_scale = shared[:, 3072:3840]
        qT = shared[0:HD, 0:NHA * S].rearrange("p (n t) -> p n t", n=NHA)
        probs = sb("probs", [P, 2, SOFT])
        pT = sb("pT", [P, SOFT])
        pooledT = [x[0:GC, :].rearrange("p (c t) -> p c t", c=8) for x in (probs[:, 1, :], pT[:, :])]
        ident = sb("ident", [P, P])
        mask = sb("mask", [P, P])
        v_mixed = sb("v_mixed", [P, KVH * HD])
        head_gain_col = sb("head_gain_col", [HD, 6])
        inv_count = sb("inv_count", [P, NT, GROUPS])
        rot_gain = sb("rot_gain", [P, 2, ROT])
        sinks = sb("sinks", [P, NHA])
        pos_i = sb("pos_i", [P, NT], I32)
        inv_freq = sb("inv_freq", [P, RH])
        rope = sb("rope", [P, 8, NT, RH])
        rot = sb("rot", [P, 4, NT * NHA * RH])
        row_ss = sb("row_ss", [P, 2 * NT])
        row_rs = sb("row_rs", [P, 2 * NT])
        row_ms = sb("row_ms", [P, 2 * NT])
        head_ss = sb("head_ss", [P, 6, 16])
        head_ms = sb("head_ms", [P, 6, 16])
        head_rs = sb("head_rs", [P, 6, 16])
        minus_half = sb("minus_half", [P, 16])
        row_max = sb("row_max", [P, 2, 8])
        neg_max = sb("neg_max", [P, 2, 8])
        sink_p = sb("sink_p", [P, 2, 8])
        den = sb("den", [P, 2, 8])
        warm = sb("warm", [P, 512], mybir.dt.bfloat16)
        table_scratch = sb("table_scratch", [P, 1])
        squares = sb("squares", [P, D], mybir.dt.bfloat16)

        x_landed = sem("x_landed")
        x1_landed = sem("x1_landed")
        mem_landed = sem("mem_landed")
        mem_again_landed = sem("mem_again_landed")
        consts_landed = sem("consts_landed")
        ident_landed = sem("ident_landed")
        gain_landed = [sem(f"gain_landed{s}") for s in range(2)]
        raw_landed = [sem(f"raw_landed{s}") for s in range(SLOTS)]
        hi_ready = [sem(f"hi_ready{s}") for s in range(SLOTS)]
        lo_ready = [sem(f"lo_ready{s}") for s in range(SLOTS)]
        weights_used = [sem(f"weights_used{s}") for s in range(SLOTS)]
        row_summed = sem("row_summed")
        row_scaled = sem("row_scaled")
        xn_ready = sem("xn_ready")
        turned = sem("turned")
        split_hi = sem("split_hi")
        split_lo = sem("split_lo")
        gu_done = sem("gu_done")
        silu_ready = sem("silu_ready")
        act_ready = sem("act_ready")
        act_turned = sem("act_turned")
        actT_hi_ready = sem("actT_hi_ready")
        actT_lo_ready = sem("actT_lo_ready")
        sum_done = sem("sum_done")
        h_ready = sem("h_ready")
        mkv_done = sem("mkv_done")
        mkv_ready = sem("mkv_ready")
        kv_done = sem("kv_done")
        kv_ready = sem("kv_ready")
        mixed_ready = sem("mixed_ready")
        warm_ready = sem("warm_ready")
        ones_ready = sem("ones_ready")
        z_done = sem("z_done")
        z_ready = sem("z_ready")
        head_summed = sem("head_summed")
        head_scaled = sem("head_scaled")
        head_ready = sem("head_ready")
        head_turned = sem("head_turned")
        headT_ready = sem("headT_ready")
        pooled_done = sem("pooled_done")
        pooled_ready = sem("pooled_ready")
        pool_y_done = sem("pool_y_done")
        pool_y_ready = sem("pool_y_ready")
        score_done = sem("score_done")
        max_ready = sem("max_ready")
        probs_ready = sem("probs_ready")
        probs_turned = sem("probs_turned")
        pT_ready = sem("pT_ready")
        o_done = sem("o_done")
        o_ready = sem("o_ready")
        angle_ready = sem("angle_ready")
        rope_ready = sem("rope_ready")
        half_ready = sem("half_ready")
        dve_step = sem("dve_step")
        pool_step = sem("pool_step")
        out_landed = sem("out_landed")

        def slot(u):
            return u % SLOTS

        def cycle(u):
            return u // SLOTS

        def product_done(eng, t, first_done, count, u):
            if t == 0:
                eng.wait_ge(first_done, count)
            else:
                eng.wait_ge(weights_used[slot(u)], cycle(u) * 2 + 2)

        sum_units = [UNIT["ffn0"] + FFN_UNITS - 1, UNIT["out0"] + 3, UNIT["ffn1"] + FFN_UNITS - 1,
                     UNIT["ffn2"] + FFN_UNITS - 1, UNIT["out1"] + 3, UNIT["ffn3"] + FFN_UNITS - 1]

        def half(w, b):
            return w[:, 2 * b:2 * b + 2, :]

        def split_index(name, t, b):
            return (SPLITS.index(name) * NT + t) * 2 + b

        def head_view(name):
            src = {"mk": mkv_sb[:, :, 0:MEMH * HD], "k": kv_sb[:, :, 0:KVH * HD],
                   "mq": xn[:, :, MIXER:D], "qa": xn[:, :, 0:8 * HD], "qm": xn[:, :, 8 * HD:D]}[name[:-1]]
            return src.rearrange("p t (n d) -> p t n d", d=HD)

        def turn_bank(t, b):
            return SUM_BANK + 2 * t + b

        def score_view(r):
            kind, t, h0, nh, width = ROUNDS[r]
            flat = ps[:, 2 * (r % 2):2 * (r % 2) + 2, :].rearrange("p b n -> p (b n)")
            return flat[:, 0:nh * width].rearrange("p (n k) -> p n k", n=nh)

        def scale_view(r):
            kind, t, h0, nh, width = ROUNDS[r]
            if r < LAYER_ROUNDS[0][1]:
                return head_rs[:, HEADNORMS.index("mq0"), t * MEMH:(t + 1) * MEMH]
            if kind == "mem":
                return head_rs[:, HEADNORMS.index("qm1"), 8 * t + 4:8 * t + 8]
            return head_rs[:, HEADNORMS.index("qa1" if h0 == 0 else "qm1"), 8 * t:8 * t + nh]

        def probs_view(r):
            kind, t, h0, nh, width = ROUNDS[r]
            return probs[:, r % 2, 0:nh * width].rearrange("p (n k) -> p n k", n=nh)

        block = ctx.enter_context(nc.Block())

        @block.sync
        def _(sp):
            w_gu = {f"ffn{f}": a[n][l].rearrange("(k p) (j f) -> p k j f", p=P, j=2) for f, (n, l) in
                    enumerate((("ffn1_w_gate_up", 0), ("ffn2_w_gate_up", 0), ("ffn1_w_gate_up", 1), ("ffn2_w_gate_up", 1)))}
            w_dn = {f"ffn{f}": a[n][l].rearrange("(c p) d -> p c d", p=P) for f, (n, l) in
                    enumerate((("ffn1_w_down", 0), ("ffn2_w_down", 0), ("ffn1_w_down", 1), ("ffn2_w_down", 1)))}
            dense = {"mkv0": a["w_mem_kv"][0], "mkv1": a["w_mem_kv"][1], "kv": a["w_kv"], "z0": a["w_in"][0],
                     "z1": a["w_in"][1], "out0": a["w_out"][0], "out1": a["w_out"][1]}

            def load(u, c, halves):
                if not isinstance(c, int) or c > 0:
                    sp.wait_ge(lo_ready[slot(u)], c * 2)
                for dst, src in halves:
                    sp.dma_start(dst, src).then_inc(raw_landed[slot(u)], 16)

            def load_gate_up(name, i):
                for j in range(2):
                    u = UNIT[name] + j
                    load(u, cycle(u) + i,
                         [(w_raw[slot(u)][:, :, g * FB:(g + 1) * FB],
                           w_gu[name][:, 4 * j:4 * j + 4, g, bass.ds(i * FB, FB)]) for g in range(2)])

            def load_down(name, i):
                u = UNIT[name] + 2
                load(u, cycle(u) + i,
                     [(half(w_raw[slot(u)], b).rearrange("p n d -> p (n d)"),
                       w_dn[name][:, bass.ds(i * 2 + b, 1), :].rearrange("p c d -> p (c d)")) for b in range(2)])

            def load_dense(name, m):
                w = dense[name].rearrange("(k p) n -> p k n", p=P)
                n, j = m // 2, m % 2
                u = UNIT[name] + m
                load(u, cycle(u), [(half(w_raw[slot(u)], b),
                                    w[:, 4 * j + 2 * b:4 * j + 2 * b + 2, n * 512:(n + 1) * 512]) for b in range(2)])

            def first_two(name):
                if name.startswith("ffn"):
                    load_gate_up(name, 0)
                else:
                    load_dense(name, 0)
                    load_dense(name, 1)

            x_dram = a["x"][0].rearrange("(t p) d -> p t d", p=P)
            sp.dma_start(h[:, 0, :], x_dram[:, 0, :]).then_inc(x_landed, 16)
            sp.dma_start(h[:, 1, :], x_dram[:, 1, :]).then_inc(x1_landed, 16)
            first_two(STAGES[0])
            sp.dma_start(ycat[:, :, :], a["mem"][0].rearrange("(t p) d -> p t d", p=P)).then_inc(mem_landed, 16)
            for name, following in zip(STAGES, STAGES[1:] + [None]):
                if name.startswith("ffn"):
                    load_gate_up(name, 1)
                    load_down(name, 0)
                    with sp.Fori(2, STEPS) as i:
                        load_gate_up(name, i)
                        load_down(name, i - 1)
                    if following is not None:
                        first_two(following)
                    load_down(name, STEPS - 1)
                else:
                    for m in range(2, dense[name].shape[1] // 256):
                        load_dense(name, m)
                    first_two(following)
            out_dram = out[0].rearrange("(t p) d -> p t d", p=P)
            for t in range(NT):
                sp.wait_ge(h_ready, 5 * NT + t + 1)
                sp.dma_start(out_dram[:, t, :], h[:, t, :]).then_inc(out_landed, 16)
            sp.wait_ge(out_landed, 16 * NT)

        gains = [a["ffn1_norm"][0], a["mem_norm"][0], a["mix_norm"][0], a["ffn2_norm"][0], a["kv_norm"],
                 a["ffn1_norm"][1], a["mem_norm"][1], a["mix_norm"][1], a["ffn2_norm"][1]]

        @block.gpsimd
        def _(pool):
            step = [0]

            def link(ins):
                step[0] += 1
                ins.then_inc(pool_step, 1)
                pool.wait_ge(pool_step, step[0])

            def load_gain(k):
                if k >= 2:
                    pool.wait_ge(xn_ready, (k - 2) * NT + NT)
                pool.dma_start(gain[:, k % 2, :], gains[k].partition_broadcast(P)).then_inc(gain_landed[k % 2], 16)

            def load_mem():
                pool.dma_start(ycat[:, :, :], a["mem"][0].rearrange("(t p) d -> p t d", p=P)).then_inc(mem_again_landed, 16)

            def row_roots(k):
                for t in range(NT):
                    c = (k % 2) * NT + t
                    pool.wait_ge(row_summed, k * NT + t + 1)
                    link(nc.gpsimd.tensor_scalar(row_ms[:, c:c + 1], row_ss[:, c:c + 1], 1.0 / D, EPS, ALU.mult, ALU.add))
                    nc.gpsimd.tensor_tensor(row_rs[:, c:c + 1], row_ms[:, c:c + 1], minus_half[:, 0:1],
                                            ALU.pow).then_inc(row_scaled, 1)

            def head_roots(name):
                x = HEADNORMS.index(name)
                n = head_view(name).shape[1] * head_view(name).shape[2]
                pool.wait_ge(head_summed, x + 1)
                share, eps = (1.0, EPS * HD) if name[0] == "q" or name[1] == "q" else (1.0 / HD, EPS)
                link(nc.gpsimd.tensor_scalar(head_ms[:, x, 0:n], head_ss[:, x, 0:n], share, eps, ALU.mult, ALU.add))
                nc.gpsimd.tensor_tensor(head_rs[:, x, 0:n], head_ms[:, x, 0:n], minus_half[:, 0:n],
                                        ALU.pow).then_inc(head_scaled, 1)

            nc.gpsimd.memset(warm[:, :], 0.0).then_inc(warm_ready, 1)
            load_gain(0)
            link(nc.gpsimd.memset(minus_half[:, :], -0.5))
            nc.gpsimd.memset(table_scratch[:, :], 0.0).then_inc(ones_ready, 1)
            nc.gpsimd.memset(head_gain_col[0:ROT, 2:3], 1.0).then_inc(ones_ready, 1)
            nc.gpsimd.memset(head_gain_col[0:ROT, 4:5], 1.0).then_inc(ones_ready, 1)
            load_gain(1)
            row_roots(0)
            row_roots(1)
            small = [
                (inv_freq[:, :], a["c_inv_freq"].partition_broadcast(P)),
                (pos_i[:, 0:1], a["positions"][0, 0:P].rearrange("(p o) -> p o", o=1)),
                (pos_i[:, 1:2], a["positions"][0, P:S].rearrange("(p o) -> p o", o=1)),
                (band0, a["c_band0"]),
                (band1, a["c_band1"]),
                (inv_count[:, :, :], a["c_inv_count"]),
                (mask[:, :], a["c_mask"]),
                (pool_w, a["pool_w"][0].rearrange("g (c p) d -> p g c d", p=GC)),
                (pool_scale, a["pool_scale"][0].partition_broadcast(P)),
                (head_gain_col[:, 0:1], a["mem_k_norm"][0].rearrange("(p o) -> p o", o=1)),
                (head_gain_col[:, 1:2], a["mem_q_norm"][0].rearrange("(p o) -> p o", o=1)),
                (head_gain_col[ROT:HD, 2:3], a["k_norm"][ROT:HD].rearrange("(p o) -> p o", o=1)),
                (head_gain_col[:, 3:4], a["mem_k_norm"][1].rearrange("(p o) -> p o", o=1)),
                (head_gain_col[ROT:HD, 4:5], a["attn_q_norm"][0, ROT:HD].rearrange("(p o) -> p o", o=1)),
                (head_gain_col[:, 5:6], a["mem_q_norm"][1].rearrange("(p o) -> p o", o=1)),
                (rot_gain[:, 0, :], a["k_norm"][0:ROT].partition_broadcast(P)),
                (rot_gain[:, 1, :], a["attn_q_norm"][0, 0:ROT].partition_broadcast(P)),
                (sinks[:, :], a["attn_sinks"][0].partition_broadcast(P)),
            ]
            assert len(small) == SMALL_LOADS
            for dst, src in small:
                pool.dma_start(dst, src).then_inc(consts_landed, 16)
            load_gain(2)
            row_roots(2)
            load_gain(3)
            head_roots("mk0")
            head_roots("mq0")
            pool.wait_ge(turned, split_index("Y0", 1, 1) + 1)
            load_mem()
            for k in (3, 4, 5, 6):
                row_roots(k)
                load_gain(k + 1)
            row_roots(7)
            load_gain(8)
            head_roots("k1")
            head_roots("mk1")
            head_roots("qa1")
            head_roots("qm1")
            row_roots(8)

        @block.scalar
        def _(act):
            def high(u, c, part=None):
                s = slot(u)
                act.wait_ge(raw_landed[s], (c + 1) * 32)
                for b in range(2) if part is None else (part,):
                    if not isinstance(c, int) or c > 0:
                        act.wait_ge(weights_used[s], c * 2 + (b - 1))
                    nc.scalar.copy(half(w_hi[s], b), half(w_raw[s], b)).then_inc(hi_ready[s], 1)

            def high_u(u):
                if u < UNITS:
                    high(u, cycle(u))

            def row_sum(k, t):
                src = h if NORMS[k][0] == "h" else ycat
                c = (k % 2) * NT + t
                if k == 0:
                    act.wait_ge(x_landed if t == 0 else x1_landed, 16)
                elif NORMS[k][0] == "mem":
                    act.wait_ge(mem_landed if k == 1 else mem_again_landed, 16)
                else:
                    act.wait_ge(h_ready, (RESID_BEFORE[k] - 1) * NT + t + 1)
                if k >= 2:
                    act.wait_ge(row_scaled, (k - 2) * NT + t + 1)
                if 2 * k + t > 0:
                    act.wait_ge(row_summed, 2 * k + t)
                nc.scalar.activation(squares[:, :], src[:, t, :], ACT.Square,
                                     accum_out=row_ss[:, c:c + 1]).then_inc(row_summed, 1)

            def split(name, t, dest):
                for b in range(2):
                    q = split_index(name, t, b)
                    act.wait_ge(turned, q + 1)
                    nc.scalar.copy(tr_hi[dest][:, 4 * b:4 * b + 4, t * P:(t + 1) * P],
                                   ps[:, turn_bank(t, b), :].rearrange("p (k t) -> p k t", k=4)).then_inc(split_hi, 1)

            def silu(c, t, u, used):
                if t == 0:
                    act.wait_ge(gu_done, c + 1)
                else:
                    act.wait_ge(weights_used[slot(u + 1)], used * 2 + 2)
                nc.scalar.activation(silu_g[:, t, :], ps[:, GU_BANK + t, 0:FB], ACT.Silu).then_inc(silu_ready, 1)

            def actT_high(e):
                act.wait_ge(act_turned, e + 1)
                nc.scalar.copy(actT_hi[:, :, :, :].rearrange("p c t n -> p (c t n)"),
                               ps[:, TR_BANK, :]).then_inc(actT_hi_ready, 1)

            def ffn(f, between=None):
                u = UNIT[f"ffn{f}"]
                c0 = f * STEPS
                e0 = f * (STEPS + 1)

                def step(c, first=False):
                    if not first:
                        high(u + 2, c - 1 + cycle(u + 2))
                    silu(c0 + c, 0, u, None)
                    if not first:
                        actT_high(e0 + c - 1)
                    high(u, c + 1 + cycle(u))
                    silu(c0 + c, 1, u, cycle(u + 1) + c)
                    high(u + 1, c + 1 + cycle(u + 1))

                step(0, first=True)
                if between is not None:
                    between()
                step(1)
                with act.Fori(2, STEPS - 1) as i:
                    step(i)
                last = STEPS - 1
                high(u + 2, last - 1 + cycle(u + 2))
                silu(c0 + last, 0, u, None)
                actT_high(e0 + last - 1)
                high_u(u + FFN_UNITS)
                silu(c0 + last, 1, u, cycle(u + 1) + last)
                high_u(u + FFN_UNITS + 1)
                for fc in range(2):
                    act.wait_ge(act_turned, e0 + last + fc + 1)
                    act.wait_ge(weights_used[slot(u + 2)], (last - 1 + cycle(u + 2)) * 2 + fc + 1)
                    nc.scalar.copy(actT_hi[:, fc, :, :].rearrange("p t n -> p (t n)"),
                                   ps[:, TR_BANK + fc, fc * FB:(fc + 1) * FB]).then_inc(actT_hi_ready, 1)
                    high(u + 2, last + cycle(u + 2), fc)

            def head_copy(y):
                name, part, bank, g = HEADTS[y]
                dst = {"mk0": mkT, "mk1": mkT, "k1": kT, "mq0": mqT, ("qm1", 1): mqT}.get(name if part == 0 else (name, part))
                first = 4 * part + (8 if name == "qm1" else 0)
                dst = qT[:, first:first + 4, :] if dst is None else dst[:, :, :]
                if y == 0:
                    act.wait_ge(consts_landed, 16 * SMALL_LOADS)
                    act.wait_ge(ones_ready, 3)
                act.wait_ge(head_turned, y + 1)
                nc.scalar.activation(dst.rearrange("p n t -> p (n t)"),
                                     ps[0:HD, bank:bank + 2, :].rearrange("p b n -> p (b n)"), ACT.Copy,
                                     scale=head_gain_col[:, g:g + 1]).then_inc(headT_ready, 1)

            def z_copy(l, n, t):
                product_done(act, t, z_done, l * 2 + n + 1, UNIT[f"z{l}"] + 2 * n + 1)
                nc.scalar.copy(xn[:, t, n * 512:(n + 1) * 512], ps[:, SUM_BANK + 2 * t + n, :]).then_inc(z_ready, 1)

            def table_of_exp():
                nc.scalar.activation(table_scratch[:, :], table_scratch[:, :], ACT.Exp)

            def exponentials(r):
                kind, t, h0, nh, width = ROUNDS[r]
                act.wait_ge(max_ready, r + 1)
                if r >= 2:
                    act.wait_ge(probs_turned, 2 * (r - 1))
                    act.wait_ge(o_ready, r - 1)
                if kind == "band":
                    nc.scalar.activation(sink_p[:, r % 2, 0:nh], sink_p[:, r % 2, 0:nh], ACT.Exp)
                for n in range(nh):
                    ins = nc.scalar.activation(probs_view(r)[:, n, :], score_view(r)[:, n, :], ACT.Exp,
                                               bias=neg_max[:, r % 2, n:n + 1], scale=scale_view(r)[:, n:n + 1],
                                               accum_out=den[:, r % 2, n:n + 1])
                    if n % (nh // 2) == nh // 2 - 1:
                        ins.then_inc(probs_ready, 1)

            def attention(l):
                r0, r1 = LAYER_ROUNDS[l]
                exponentials(r0)
                if l == 1:
                    head_copy(6)
                    head_copy(7)
                for r in range(r0 + 1, r1):
                    exponentials(r)

            def proj_high(name, m):
                for j in range(m):
                    high_u(UNIT[name] + 2 + j)

            act.dma_start(ident[:, :], a["c_ident"]).then_inc(ident_landed, 16)
            row_sum(0, 0)
            row_sum(0, 1)
            split("N0", 0, "main")
            high_u(0)
            split("N0", 1, "main")
            high_u(1)
            row_sum(1, 0)
            row_sum(1, 1)

            def split_mem(name):
                split(name, 0, "side")
                split(name, 1, "side")

            def sines():
                act.wait_ge(angle_ready, 1)
                nc.scalar.activation(rope[:, 6, :, :], rope[:, 4, :, :], ACT.Sin)
                nc.scalar.activation(rope[:, 7, :, :], rope[:, 5, :, :], ACT.Sin).then_inc(rope_ready, 1)

            ffn(0, lambda: split_mem("N1"))
            row_sum(2, 0)
            row_sum(2, 1)
            proj_high("mkv0", 2)
            split("N2", 0, "main")
            split("N2", 1, "main")
            high_u(UNIT["z0"] + 2)
            z_copy(0, 0, 0)
            high_u(UNIT["z0"] + 3)
            z_copy(0, 0, 1)
            high_u(UNIT["z0"] + 4)
            head_copy(0)
            z_copy(0, 1, 0)
            high_u(UNIT["z0"] + 5)
            z_copy(0, 1, 1)
            for c in range(4):
                act.wait_ge(pooled_done, c + 1)
                both = ps[0:GC, GU_BANK + c, :].rearrange("p (c t n) -> p c t n", c=2, t=NT)
                for t in range(NT):
                    nc.scalar.copy(pooledT[t][:, 2 * c:2 * c + 2, :], both[:, :, t, :]).then_inc(pooled_ready, 1)
            head_copy(1)
            table_of_exp()
            attention(0)
            split("Y0", 0, "main")
            split("Y0", 1, "main")
            proj_high("out0", 3)
            row_sum(3, 0)
            high_u(UNIT["out0"] + 5)
            split("N3", 0, "main")
            row_sum(3, 1)
            split("N3", 1, "main")
            ffn(1, sines)
            row_sum(4, 0)
            row_sum(4, 1)
            split("N4", 0, "side")
            split("N4", 1, "side")
            row_sum(5, 0)
            row_sum(5, 1)
            row_sum(6, 0)
            row_sum(6, 1)
            proj_high("kv", 2)
            split("N5", 0, "main")
            split("N5", 1, "main")

            def split_mem_again():
                product_done(act, 1, None, None, UNIT["kv"] + 1)
                split_mem("N6")

            ffn(2, split_mem_again)
            row_sum(7, 0)
            row_sum(7, 1)
            proj_high("mkv1", 2)
            split("N7", 0, "main")
            split("N7", 1, "main")
            high_u(UNIT["z1"] + 2)
            z_copy(1, 0, 0)
            high_u(UNIT["z1"] + 3)
            z_copy(1, 0, 1)
            high_u(UNIT["z1"] + 4)
            z_copy(1, 1, 0)
            head_copy(2)
            head_copy(3)
            high_u(UNIT["z1"] + 5)
            z_copy(1, 1, 1)
            head_copy(4)
            head_copy(5)
            table_of_exp()
            attention(1)
            split("Y1", 0, "main")
            split("Y1", 1, "main")
            proj_high("out1", 3)
            row_sum(8, 0)
            high_u(UNIT["out1"] + 5)
            split("N8", 0, "main")
            row_sum(8, 1)
            split("N8", 1, "main")
            ffn(3)

        @block.vector
        def _(dve):
            step_count = [0]

            def link(ins):
                step_count[0] += 1
                ins.then_inc(dve_step, 1)
                dve.wait_ge(dve_step, step_count[0])

            def low(u, c, part=None):
                s = slot(u)
                for b in range(2) if part is None else (part,):
                    dve.wait_ge(hi_ready[s], c * 2 + (b + 1))
                    nc.vector.tensor_tensor(half(w_lo[s], b), half(w_raw[s], b), half(w_hi[s], b).bitcast(F32),
                                            ALU.subtract).then_inc(lo_ready[s], 1)

            def low_u(u):
                if u < UNITS:
                    low(u, cycle(u))

            def norm_rows(k, t):
                src = h if NORMS[k][0] == "h" else ycat
                c = (k % 2) * NT + t
                name = f"N{k}"
                if t == 0:
                    dve.wait_ge(gain_landed[k % 2], 16 * (k // 2 + 1))
                dve.wait_ge(row_scaled, k * NT + t + 1)
                q = split_index(name, t, 0)
                if q >= 2 * NT:
                    dve.wait_ge(turned, q - 2 * NT + 2)
                nc.vector.scalar_tensor_tensor(out=xn[:, t, :], in0=src[:, t, :], scalar=row_rs[:, c:c + 1],
                                               in1=gain[:, k % 2, :], op0=ALU.mult, op1=ALU.mult).then_inc(xn_ready, 1)

            def split(name, t, dest):
                for b in range(2):
                    q = split_index(name, t, b)
                    hi = tr_hi[dest][:, 4 * b:4 * b + 4, t * P:(t + 1) * P]
                    lo = tr_lo[dest][:, 4 * b:4 * b + 4, t * P:(t + 1) * P]
                    dve.wait_ge(split_hi, q + 1)
                    nc.vector.tensor_tensor(lo, ps[:, turn_bank(t, b), :].rearrange("p (k t) -> p k t", k=4),
                                            hi.bitcast(F32), ALU.subtract).then_inc(split_lo, 1)

            def gated(c, t, turned_before):
                dve.wait_ge(silu_ready, c * 2 + (t + 1))
                if turned_before is not None:
                    dve.wait_ge(act_turned, turned_before)
                nc.vector.tensor_tensor(act_f[:, t, :], ps[:, GU_BANK + t, FB:2 * FB], silu_g[:, t, :],
                                        ALU.mult).then_inc(act_ready, 1)

            def actT_low(e):
                dve.wait_ge(actT_hi_ready, e + 1)
                nc.vector.tensor_tensor(actT_lo[:, :, :, :].rearrange("p c t n -> p (c t n)"), ps[:, TR_BANK, :],
                                        actT_hi[:, :, :, :].rearrange("p c t n -> p (c t n)").bitcast(F32),
                                        ALU.subtract).then_inc(actT_lo_ready, 1)

            def ffn(f, between=None):
                u = UNIT[f"ffn{f}"]
                c0 = f * STEPS

                e0 = f * (STEPS + 1)

                def step(c, first=False):
                    if not first:
                        low(u + 2, c - 1 + cycle(u + 2))
                    gated(c0 + c, 0, None if first else e0 + c)
                    if not first:
                        actT_low(e0 + c - 1)
                    low(u, c + 1 + cycle(u))
                    gated(c0 + c, 1, None)
                    low(u + 1, c + 1 + cycle(u + 1))

                step(0, first=True)
                if between is not None:
                    between()
                step(1)
                with dve.Fori(2, STEPS - 1) as i:
                    step(i)
                last = STEPS - 1
                low(u + 2, last - 1 + cycle(u + 2))
                gated(c0 + last, 0, e0 + last)
                actT_low(e0 + last - 1)
                low_u(u + FFN_UNITS)
                gated(c0 + last, 1, None)
                low_u(u + FFN_UNITS + 1)
                for fc in range(2):
                    dve.wait_ge(actT_hi_ready, e0 + last + fc + 1)
                    nc.vector.tensor_tensor(actT_lo[:, fc, :, :].rearrange("p t n -> p (t n)"),
                                            ps[:, TR_BANK + fc, fc * FB:(fc + 1) * FB],
                                            actT_hi[:, fc, :, :].rearrange("p t n -> p (t n)").bitcast(F32),
                                            ALU.subtract).then_inc(actT_lo_ready, 1)
                    low(u + 2, last + cycle(u + 2), fc)

            def residual(r, weight, tiles=(0, 1)):
                for t in tiles:
                    product_done(dve, t, sum_done, r + 1, sum_units[r])
                    nc.vector.scalar_tensor_tensor(
                        out=h[:, t, :], in0=ps[:, SUM_BANK + 2 * t:SUM_BANK + 2 * t + 2, :].rearrange("p b n -> p (b n)"),
                        scalar=weight, in1=h[:, t, :], op0=ALU.mult, op1=ALU.add).then_inc(h_ready, 1)

            def proj_low(name, m):
                for j in range(m):
                    low_u(UNIT[name] + 2 + j)

            def kv_copy(dst, done, ready, base, name):
                for t in range(NT):
                    product_done(dve, t, done, base // NT + 1, UNIT[name] + 1)
                    nc.vector.tensor_copy(dst[:, t, :], ps[:, GU_BANK + t, :]).then_inc(ready, 1)
                dve.wait_ge(ready, base + NT)

            def head_norm(name):
                x = HEADNORMS.index(name)
                v = head_view(name)
                nt, nh = v.shape[1], v.shape[2]
                n = nt * nh
                sq = probs[:, 0, 0:n * HD].rearrange("p (n d) -> p n d", d=HD)
                rs = head_rs[:, x, 0:n].rearrange("p (t n) -> p t n", t=nt).unsqueeze(3).to_broadcast([P, nt, nh, HD])
                link(nc.vector.tensor_tensor(sq.rearrange("p (t n) d -> p t n d", t=nt), v, v, ALU.mult))
                nc.vector.tensor_reduce(head_ss[:, x, 0:n], sq, AX.X, ALU.add).then_inc(head_summed, 1)
                if name[:-1] in ("mk", "k"):
                    dve.wait_ge(head_scaled, x + 1)
                    ins = nc.vector.tensor_tensor(v, v, rs, ALU.mult)
                    if name[:-1] == "mk":
                        ins.then_inc(head_ready, 1)
                        return
                    link(ins)
                if name == "mq0":
                    return
                nh = min(nh, 4) if name == "qm1" else nh
                n = nt * nh
                v = v[:, :, 0:nh, :]
                g = rot_gain[:, 0 if name == "k1" else 1, :].unsqueeze(1).unsqueeze(1).to_broadcast([P, nt, nh, ROT])
                link(nc.vector.tensor_tensor(v[:, :, :, 0:ROT], v[:, :, :, 0:ROT], g, ALU.mult))
                x1, x2 = v[:, :, :, 0:RH], v[:, :, :, RH:ROT]
                cos, sin = (rope[:, i, :, :].unsqueeze(2).to_broadcast([P, nt, nh, RH]) for i in (6, 7))
                tmp = [rot[:, i, 0:n * RH].rearrange("p (t n d) -> p t n d", t=nt, n=nh) for i in range(4)]
                nc.vector.tensor_tensor(tmp[0], x1, cos, ALU.mult)
                nc.vector.tensor_tensor(tmp[1], x2, sin, ALU.mult)
                nc.vector.tensor_tensor(tmp[2], x2, cos, ALU.mult)
                link(nc.vector.tensor_tensor(tmp[3], x1, sin, ALU.mult))
                link(nc.vector.tensor_tensor(x1, tmp[0], tmp[1], ALU.subtract))
                nc.vector.tensor_tensor(x2, tmp[2], tmp[3], ALU.add).then_inc(head_ready, 1)

            def rope_tables():
                dve.wait_ge(consts_landed, 16 * SMALL_LOADS)
                pos, ang, whole, part, to_cos, to_sin = (rope[:, i, :, :] for i in range(6))
                posf = pos.rearrange("p t d -> p (t d)")[:, 0:NT]
                q1, q2, q3 = two_pi_parts()
                link(nc.vector.tensor_copy(posf, pos_i[:, :]))
                link(nc.vector.tensor_tensor(ang, posf.unsqueeze(2).to_broadcast([P, NT, RH]),
                                             inv_freq[:, :].unsqueeze(1).to_broadcast([P, NT, RH]), ALU.mult))
                link(nc.vector.tensor_scalar(whole, ang, 1.0 / (4096 * 2 * np.pi), MAGIC, ALU.mult, ALU.add))
                link(nc.vector.tensor_scalar(whole, whole, -MAGIC, 4096.0, ALU.add, ALU.mult))

                def less(turns, q):
                    link(nc.vector.scalar_tensor_tensor(out=ang, in0=turns, scalar=-q, in1=ang, op0=ALU.mult, op1=ALU.add))

                less(whole, q1)
                less(whole, q2)
                link(nc.vector.tensor_scalar(part, ang, 1.0 / (2 * np.pi), MAGIC, ALU.mult, ALU.add))
                link(nc.vector.tensor_scalar(part, part, -MAGIC, None, ALU.add))
                less(part, q1)
                less(part, q2)
                less(whole, q3)
                less(part, q3)
                link(nc.vector.tensor_scalar(to_sin, ang, 3.1415925, -3.1415925, ALU.min, ALU.max))
                link(nc.vector.tensor_scalar(part, to_sin, -1.0, None, ALU.mult))
                link(nc.vector.tensor_tensor(to_cos, part, to_sin, ALU.min))
                nc.vector.tensor_scalar(to_cos, to_cos, float(np.pi / 2), None, ALU.add).then_inc(angle_ready, 1)

            def maxima(r):
                kind, t, h0, nh, width = ROUNDS[r]
                mx, neg = row_max[:, r % 2, 0:nh], neg_max[:, r % 2, 0:nh]
                dve.wait_ge(score_done, r + 1)
                if r >= 2:
                    dve.wait_ge(probs_ready, 2 * (r - 1))
                link(nc.vector.tensor_reduce(mx, score_view(r), AX.X, ALU.max))
                dve.wait_ge(head_scaled, 2 if r < LAYER_ROUNDS[0][1] else 5 if (kind, h0) == ("band", 0) else 6)
                if kind == "band":
                    s = sinks[:, h0:h0 + nh]
                    link(nc.vector.tensor_tensor(mx, mx, scale_view(r), ALU.mult))
                    link(nc.vector.tensor_tensor(mx, mx, s, ALU.max))
                    nc.vector.tensor_tensor(sink_p[:, r % 2, 0:nh], s, mx, ALU.subtract)
                    nc.vector.tensor_scalar(neg, mx, -1.0, None, ALU.mult).then_inc(max_ready, 1)
                else:
                    nc.vector.scalar_tensor_tensor(out=neg, in0=mx, scalar=-1.0, in1=scale_view(r), op0=ALU.mult,
                                                   op1=ALU.mult).then_inc(max_ready, 1)

            def probs_copy(r):
                kind, t, h0, nh, width = ROUNDS[r]
                dn = den[:, r % 2, 0:nh]
                if r > 0:
                    dve.wait_ge(o_done, r)
                part = nh * width // 2
                for b in range(2):
                    dve.wait_ge(probs_turned, 2 * r + b + 1)
                    nc.vector.tensor_copy(pT[:, b * part:(b + 1) * part], ps[:, PT_BANK + b, 0:part]).then_inc(pT_ready, 1)
                dve.wait_ge(probs_ready, 2 * r + 2)
                if kind == "band":
                    link(nc.vector.tensor_tensor(dn, dn, sink_p[:, r % 2, 0:nh], ALU.add))
                link(nc.vector.reciprocal(dn, dn))

            def output(r):
                kind, t, h0, nh, width = ROUNDS[r]
                base = h0 * HD + (MIXER if kind == "mem" else 0)
                dve.wait_ge(o_done, r + 1)
                nc.vector.tensor_tensor(
                    ycat[:, t, base:base + nh * HD].rearrange("p (n d) -> p n d", d=HD),
                    ps[:, O_BANK + r % 2, 0:nh * HD].rearrange("p (n d) -> p n d", d=HD),
                    den[:, r % 2, 0:nh].unsqueeze(2).to_broadcast([P, nh, HD]), ALU.mult).then_inc(o_ready, 1)

            def attention(l, after_maxima=None):
                r0, r1 = LAYER_ROUNDS[l]
                maxima(r0)
                maxima(r0 + 1)
                if after_maxima is not None:
                    after_maxima()
                for r in range(r0, r1):
                    probs_copy(r)
                    if r + 2 < r1:
                        maxima(r + 2)
                    if r == r1 - 1:
                        split(f"Y{l}", 0, "main")
                    output(r)

            norm_rows(0, 0)
            norm_rows(0, 1)
            split("N0", 0, "main")
            low_u(0)
            split("N0", 1, "main")
            low_u(1)
            norm_rows(1, 0)
            norm_rows(1, 1)

            def split_mem(name):
                split(name, 0, "side")
                split(name, 1, "side")

            ffn(0, lambda: split_mem("N1"))
            residual(0, 0.5)
            norm_rows(2, 0)
            norm_rows(2, 1)
            proj_low("mkv0", 2)
            kv_copy(mkv_sb, mkv_done, mkv_ready, 0, "mkv0")
            split("N2", 0, "main")
            split("N2", 1, "main")
            head_norm("mk0")
            proj_low("z0", 4)
            dve.wait_ge(z_ready, 2 * NT)
            head_norm("mq0")

            def pool_output(t):
                for g in range(GROUPS):
                    dve.wait_ge(pool_y_done, t + 1)
                    nc.vector.scalar_tensor_tensor(
                        out=ycat[:, t, g * GW:(g + 1) * GW],
                        in0=ps[:, GU_BANK + 2 * t + g // 2, (g % 2) * GW:(g % 2 + 1) * GW],
                        scalar=inv_count[:, t, g:g + 1], in1=pool_scale[:, g * GW:(g + 1) * GW],
                        op0=ALU.mult, op1=ALU.mult).then_inc(pool_y_ready, 1)

            pool_output(0)
            attention(0, lambda: pool_output(1))
            split("Y0", 1, "main")
            proj_low("out0", 3)
            residual(1, 1.0, (0,))
            norm_rows(3, 0)
            low_u(UNIT["out0"] + 5)
            split("N3", 0, "main")
            residual(1, 1.0, (1,))
            norm_rows(3, 1)
            split("N3", 1, "main")
            ffn(1, rope_tables)
            residual(2, 0.5)
            norm_rows(4, 0)
            norm_rows(4, 1)
            split("N4", 0, "side")
            split("N4", 1, "side")
            norm_rows(5, 0)
            norm_rows(5, 1)
            proj_low("kv", 2)
            kv_copy(kv_sb, kv_done, kv_ready, 0, "kv")
            split("N5", 0, "main")
            split("N5", 1, "main")
            norm_rows(6, 0)
            norm_rows(6, 1)
            nc.vector.tensor_copy(v_mixed[0:CHUNK, :], kv_sb[0:CHUNK, 1, 256:512]).then_inc(mixed_ready, 1)
            nc.vector.tensor_copy(v_mixed[CHUNK:P, :], kv_sb[CHUNK:P, 0, 256:512]).then_inc(mixed_ready, 1)
            ffn(2, lambda: split_mem("N6"))
            residual(3, 0.5)
            norm_rows(7, 0)
            norm_rows(7, 1)
            proj_low("mkv1", 2)
            kv_copy(mkv_sb, mkv_done, mkv_ready, NT, "mkv1")
            split("N7", 0, "main")
            split("N7", 1, "main")
            low_u(UNIT["z1"] + 2)
            dve.wait_ge(rope_ready, 1)
            head_norm("k1")
            head_norm("mk1")
            low_u(UNIT["z1"] + 3)
            low_u(UNIT["z1"] + 4)
            dve.wait_ge(z_ready, 3 * NT)
            head_norm("qa1")
            low_u(UNIT["z1"] + 5)
            dve.wait_ge(z_ready, 4 * NT)
            head_norm("qm1")
            attention(1)
            split("Y1", 1, "main")
            proj_low("out1", 3)
            residual(4, 1.0, (0,))
            norm_rows(8, 0)
            low_u(UNIT["out1"] + 5)
            split("N8", 0, "main")
            residual(4, 1.0, (1,))
            norm_rows(8, 1)
            split("N8", 1, "main")
            ffn(3)
            residual(5, 0.5)

        @block.tensor
        def _(pe):
            def turn(name, src, ready, value, tiles=(0, 1)):
                for t in tiles:
                    pe.wait_ge(ready, value(t))
                    for b in range(2):
                        for k in range(4):
                            c = (4 * b + k) * P
                            mm = pe.transpose(ps[:, turn_bank(t, b), k * P:(k + 1) * P], src[:, t, c:c + P], ident[:, :])
                        mm.then_inc(turned, 1)

            def turn_norm(k, tiles=(0, 1)):
                turn(f"N{k}", xn, xn_ready, lambda t: k * NT + t + 1, tiles)

            def three(dst, x_hi, x_lo, wh, wl, start, stop):
                pe.matmul(dst, x_hi, wh, start=start, stop=False)
                pe.matmul(dst, x_hi, wl, start=False, stop=False)
                return pe.matmul(dst, x_lo, wh, start=False, stop=stop)

            def product(u, c, t, dst, src, split_name, wait_src, before_last=None):
                for k in range(KC):
                    s = slot(u + k // 4)
                    kk = k % 4
                    if k == KC - 1 and before_last is not None:
                        before_last()
                    if wait_src and k % 4 == 0:
                        pe.wait_ge(split_lo, split_index(split_name, t, k // 4) + 1)
                    if t == 0 and kk % 2 == 0:
                        pe.wait_ge(lo_ready[s], c[k // 4] * 2 + (kk // 2 + 1))
                    mm = three(dst, tr_hi[src][:, k, t * P:(t + 1) * P], tr_lo[src][:, k, t * P:(t + 1) * P],
                               w_hi[s][:, kk, :], w_lo[s][:, kk, :], k == 0, k == KC - 1)
                    if t == NT - 1 and kk % 2 == 1:
                        if k == KC - 1:
                            return mm, s
                        mm.then_inc(weights_used[s], 1)
                return mm, None

            def projection(name, src, split_name, bank, done, order, blocks=None, tiles=(0, 1), before_last=None):
                if blocks is None:
                    blocks = range(2) if name in ("z0", "z1", "out0", "out1") else range(1)
                for n in blocks:
                    for t in tiles:
                        u = UNIT[name] + 2 * n
                        mm, s = product(u, (cycle(u), cycle(u + 1)), t, ps[:, bank(t, n), :], src, split_name, n == 0,
                                        before_last if n == blocks[-1] and t == NT - 1 else None)
                        if s is not None:
                            mm.then_inc(weights_used[s], 1)
                        elif order(n):
                            mm.then_inc(done, 1)

            def ffn(f, norm, mem_norm=None):
                split_name = f"N{norm}"
                u = UNIT[f"ffn{f}"]
                c0 = f * STEPS
                e0 = f * (STEPS + 1)

                def gate_up(c, t, first=False, before_last=None):
                    if not first or f > 0:
                        pe.wait_ge(act_ready, (c0 + c) * 2 + (t - 1))
                    mm, s = product(u, (cycle(u) + c, cycle(u + 1) + c), t, ps[:, GU_BANK + t, :], "main", split_name, first,
                                    before_last)
                    mm.then_inc(gu_done if s is None else weights_used[s], 1)

                def turn_act(c, split=False):
                    pe.wait_ge(act_ready, (c0 + c) * 2 + 2)
                    for fc in range(2):
                        bank = TR_BANK + (fc if split else 0)
                        for t in range(NT):
                            mm = pe.transpose(ps[:, bank, (fc * NT + t) * P:(fc * NT + t + 1) * P],
                                              act_f[:, t, fc * P:(fc + 1) * P], ident[:, :])
                        if split or fc == 1:
                            mm.then_inc(act_turned, 1)

                def down(c, fc, parts, first=False, last=False):
                    s = slot(u + 2)
                    if parts == 2 or fc == 0:
                        pe.wait_ge(actT_lo_ready, e0 + c + (1 + (fc if parts == 2 else 0)))
                    pe.wait_ge(lo_ready[s], (cycle(u + 2) + c) * 2 + (fc + 1))
                    for t in range(NT):
                        xh, xl = actT_hi[:, fc, t, :], actT_lo[:, fc, t, :]
                        wh = [w_hi[s][:, 2 * fc + n, :] for n in range(2)]
                        wl = [w_lo[s][:, 2 * fc + n, :] for n in range(2)]
                        dst = [ps[:, SUM_BANK + 2 * t + n, :] for n in range(2)]
                        for n in range(2):
                            pe.matmul(dst[n], xh, wh[n], start=first and fc == 0, stop=False)
                        for n in range(2):
                            pe.matmul(dst[n], xh, wl[n], start=False, stop=False)
                        for n in range(2):
                            mm = pe.matmul(dst[n], xl, wh[n], start=False, stop=last and fc == 1)
                        if t == NT - 1:
                            mm.then_inc(weights_used[s], 1)
                        elif last and fc == 1:
                            mm.then_inc(sum_done, 1)

                gate_up(0, 0, first=True, before_last=(lambda: turn_norm(norm, (1,))) if f % 2 == 1 else None)
                gate_up(0, 1, first=True)
                gate_up(1, 0)
                turn_act(0)
                if mem_norm is not None:
                    turn_norm(mem_norm)
                gate_up(1, 1)
                if mem_norm is not None:
                    pe.wait_ge(split_lo, split_index(f"N{mem_norm}", 1, 1) + 1)
                down(0, 0, 1, first=True)
                down(0, 1, 1)
                last = STEPS - 1
                with pe.Fori(2, last) as i:
                    gate_up(i, 0)
                    turn_act(i - 1)
                    gate_up(i, 1)
                    down(i - 1, 0, 1)
                    down(i - 1, 1, 1)
                gate_up(last, 0)
                turn_act(last - 1)
                gate_up(last, 1)
                down(last - 1, 0, 1)
                turn_act(last, split=True)
                down(last - 1, 1, 1)
                down(last, 0, 2)
                down(last, 1, 2, last=True)

            def turn_heads(y):
                name, part, bank, _ = HEADTS[y]
                v = head_view(name)
                if name == "mq0":
                    pe.wait_ge(z_ready, 2 * NT)
                else:
                    pe.wait_ge(head_ready, HEADREADY.index(name) + 1)
                if y >= 2:
                    pe.wait_ge(headT_ready, y - 1)
                dst = ps[0:HD, bank:bank + 2, :].rearrange("p b (n t k) -> p (b n) t k", n=2, t=NT)
                for n in range(4):
                    for t in range(NT):
                        mm = pe.transpose(dst[:, n, t, :], v[:, t, 4 * part + n, :], ident[:, :])
                mm.then_inc(head_turned, 1)

            def scores(r):
                kind, t, h0, nh, width = ROUNDS[r]
                dst = score_view(r)
                if r - 2 >= 0:
                    pe.wait_ge(probs_ready, 2 * (r - 1))
                if kind == "band" and t == 0:
                    for n in range(0, nh, 4):
                        pe.matmul(dst[:, n:n + 4, :], ident[:, :], mask[:, :].unsqueeze(1).to_broadcast([P, 4, P]),
                                  start=True, stop=False)
                for n in range(nh):
                    if kind == "mem":
                        mm = pe.matmul(dst[:, n, :], mqT[:, n, t * P:(t + 1) * P], mkT[:, n, :], start=True, stop=True)
                        continue
                    q, k = qT[:, h0 + n, :], kT[:, (h0 + n) // GQA, :]
                    if t == 0:
                        mm = pe.matmul(dst[:, n, :], q[:, 0:P], k[:, 0:P], start=False, stop=(n % 4 == 3))
                    else:
                        pe.matmul(dst[0:CHUNK, n, 0:CHUNK], q[:, P:P + CHUNK], k[:, P:P + CHUNK], start=True, stop=True)
                        pe.matmul(dst[0:CHUNK, n, CHUNK:P], q[:, P:P + CHUNK], k[:, CHUNK:P], start=True, stop=True)
                        mm = pe.matmul(dst[CHUNK:P, n, :], q[:, P + CHUNK:S], k[:, P:S], start=True, stop=True)
                mm.then_inc(score_done, 1)

            def turn_probs(r):
                kind, t, h0, nh, width = ROUNDS[r]
                blocks = nh * width // P // 2
                for b in range(2):
                    pe.wait_ge(probs_ready, 2 * r + b + 1)
                    if r > 0:
                        pe.wait_ge(pT_ready, 2 * (r - 1) + b + 1)
                    for j in range(blocks):
                        c = (b * blocks + j) * P
                        mm = pe.transpose(ps[:, PT_BANK + b, j * P:(j + 1) * P], probs[:, r % 2, c:c + P], ident[:, :])
                    mm.then_inc(probs_turned, 1)

            def values(r):
                kind, t, h0, nh, width = ROUNDS[r]
                if r >= 2:
                    pe.wait_ge(o_ready, r - 1)
                for n in range(nh):
                    if n % (nh // 2) == 0:
                        pe.wait_ge(pT_ready, 2 * r + n // (nh // 2) + 1)
                    dst = ps[:, O_BANK + r % 2, n * HD:(n + 1) * HD]
                    if kind == "mem":
                        v = mkv_sb[:, :, 256 + n * HD:256 + (n + 1) * HD]
                        for b in range(2):
                            j = (2 * n + b) * P
                            mm = pe.matmul(dst, pT[:, j:j + P], v[:, b, :], start=(b == 0), stop=(b == 1))
                        continue
                    g = (h0 + n) // GQA * HD
                    v = kv_sb[:, t, 256 + g:256 + g + HD]
                    if t == 0:
                        mm = pe.matmul(dst, pT[:, n * P:(n + 1) * P], v, start=True, stop=True)
                    else:
                        pe.matmul(dst[0:CHUNK, :], pT[:, n * P:n * P + CHUNK], v_mixed[:, g:g + HD], start=True, stop=True)
                        mm = pe.matmul(dst[CHUNK:P, :], pT[:, n * P + CHUNK:(n + 1) * P], v, start=True, stop=True)
                mm.then_inc(o_done, 1)

            def attention(l, scored=False):
                r0, r1 = LAYER_ROUNDS[l]
                if not scored:
                    scores(r0)
                    scores(r0 + 1)
                for r in range(r0, r1):
                    turn_probs(r)
                    if l == 1 and r == r0:
                        pe.wait_ge(headT_ready, len(HEADTS))
                    if r + 2 < r1:
                        scores(r + 2)
                    if r == r1 - 1:
                        turn(f"Y{l}", ycat, o_ready, lambda t: r1 - 1, (0,))
                    values(r)
                turn(f"Y{l}", ycat, o_ready, lambda t: r1, (1,))

            def pooled(c0, c1):
                for c in range(c0, c1):
                    dst = ps[0:GC, GU_BANK + c // 2, (c % 2) * S:(c % 2 + 1) * S]
                    cols = slice(c * GC, (c + 1) * GC)
                    pe.matmul(dst, xn[:, 0, cols], band0[:, c // 2, :], start=True, stop=False)
                    mm = pe.matmul(dst[:, P:S], xn[:, 1, cols], band1[:, c // 2, :], start=False, stop=True)
                    if c % 2 == 1:
                        mm.then_inc(pooled_done, 1)

            def pool_products(tiles):
                pe.wait_ge(pooled_ready, 4 * NT)
                for t in tiles:
                    for g in range(GROUPS):
                        dst = ps[:, GU_BANK + 2 * t + g // 2, (g % 2) * GW:(g % 2 + 1) * GW]
                        for c in range(2):
                            mm = pe.matmul(dst, pooledT[t][:, 2 * g + c, :], pool_w[:, g, c, :],
                                           start=(c == 0), stop=(c == 1))
                    mm.then_inc(pool_y_done, 1)

            def to_gu(t, n):
                return GU_BANK + t

            def to_sum(t, n):
                return SUM_BANK + 2 * t + n

            pe.wait_ge(warm_ready, 1)
            for _ in range(WARM_PRODUCTS):
                pe.matmul(ps[:, GU_BANK, :], warm[:, 0:P], warm[:, :], start=True, stop=True)
            pe.wait_ge(ident_landed, 16)
            turn_norm(0)
            ffn(0, 0, mem_norm=1)
            projection("mkv0", "side", "N1", to_gu, mkv_done, lambda n: True)
            turn_norm(2)
            pe.wait_ge(h_ready, NT)
            z0 = ("z0", "main", "N2", to_sum, z_done, lambda n: True)
            projection(*z0, blocks=(0,))
            turn_heads(0)
            projection(*z0, blocks=(1,), tiles=(0,))
            pe.wait_ge(consts_landed, 16 * SMALL_LOADS)
            pe.wait_ge(z_ready, NT)
            pe.wait_ge(mkv_ready, NT)
            pooled(0, 4)
            projection(*z0, blocks=(1,), tiles=(1,))
            pe.wait_ge(headT_ready, 1)
            pe.wait_ge(z_ready, 2 * NT)
            pooled(4, 8)
            turn_heads(1)
            pool_products((0,))
            pe.wait_ge(headT_ready, 2)
            r0 = LAYER_ROUNDS[0][0]
            scores(r0)
            scores(r0 + 1)
            pool_products((1,))
            pe.wait_ge(pool_y_ready, NT * GROUPS)
            attention(0, scored=True)
            projection("out0", "main", "Y0", to_sum, sum_done, lambda n: n == 1, before_last=lambda: turn_norm(3, (0,)))
            ffn(1, 3)
            turn_norm(4)
            projection("kv", "side", "N4", to_gu, kv_done, lambda n: True)
            turn_norm(5)
            pe.wait_ge(kv_ready, NT)
            ffn(2, 5, mem_norm=6)
            projection("mkv1", "side", "N6", to_gu, mkv_done, lambda n: True)
            turn_norm(7)
            pe.wait_ge(h_ready, 4 * NT)
            z1 = ("z1", "main", "N7", to_sum, z_done, lambda n: True)
            projection(*z1, blocks=(0,))
            pe.wait_ge(mkv_ready, 2 * NT)
            projection(*z1, blocks=(1,), tiles=(0,))
            turn_heads(2)
            turn_heads(3)
            projection(*z1, blocks=(1,), tiles=(1,))
            turn_heads(4)
            turn_heads(5)
            pe.wait_ge(headT_ready, 6)
            pe.wait_ge(z_ready, 4 * NT)
            r0 = LAYER_ROUNDS[1][0]
            scores(r0)
            scores(r0 + 1)
            turn_heads(6)
            turn_heads(7)
            pe.wait_ge(headT_ready, len(HEADTS) - 1)
            pe.wait_ge(mixed_ready, 2)
            attention(1, scored=True)
            projection("out1", "main", "Y1", to_sum, sum_done, lambda n: n == 1, before_last=lambda: turn_norm(8, (0,)))
            ffn(3, 8)


_INS = ['x', 'mem', 'positions', 'ffn1_norm', 'ffn1_w_gate_up', 'ffn1_w_down', 'mix_norm', 'w_in', 'w_out',
        'pool_w', 'pool_scale', 'attn_q_norm', 'attn_sinks', 'kv_norm', 'w_kv', 'k_norm',
        'mem_norm', 'w_mem_kv', 'mem_q_norm', 'mem_k_norm', 'ffn2_norm', 'ffn2_w_gate_up', 'ffn2_w_down']


def kernel(**inputs):
    import numpy as _np
    import concourse.bacc as _bacc
    from concourse import mybir as _mybir
    from concourse.bass_utils import run_bass_kernel_spmd as _run

    nc = _bacc.Bacc("TRN2", target_bir_lowering=False, num_devices=1)
    arrays, aps = {}, {}
    for name, value in [(n, inputs[n]) for n in _INS] + list(shape_constants().items()):
        v = _np.ascontiguousarray(value)
        arrays[f"in_{name}_dram"] = v
        aps[name] = nc.dram_tensor(f"in_{name}_dram", v.shape, _mybir.dt.from_np(v.dtype), kind="ExternalInput").ap()
    out = nc.dram_tensor("out_0_dram", (1, S, D), _mybir.dt.float32, kind="ExternalOutput").ap()
    encoder_kernel(nc, aps, out)
    r = _run(nc, [arrays], core_ids=[0])
    return r.results[0]["out_0_dram"]
```
